# Optimizing a Trainium2 kernel written in Bass

```python
import jax, jax.numpy as jnp
from jax import lax
import numpy as np

D_MODEL = 2048
BATCH = 1
SEQ = 512
DEPTH = 1

CHUNK = 64
WINDOW = 128
WINDOW_CHUNKS = WINDOW // CHUNK
ROPE_THETA = 10000.0
EPS = 1e-6
Q_BLOCK = 128
MASK_VALUE = -1e30

A_HEADS = 16
A_KV_HEADS = 2
A_HEAD_DIM = 64
A_WIDTH = A_HEADS * A_HEAD_DIM

B_HEADS = 8
B_Q_LORA = 512
B_KV_LORA = 256
B_NOPE = 128
B_ROPE = 64
B_V = 128
B_WIDTH = B_HEADS * B_V

MIX_WIDTH = A_WIDTH + B_WIDTH

A_Q_COLS = A_WIDTH
A_K_COLS = A_KV_HEADS * A_HEAD_DIM
A_V_COLS = A_KV_HEADS * A_HEAD_DIM
A_G_COLS = A_WIDTH
B_CQ_COLS = B_Q_LORA
B_CKV_COLS = B_KV_LORA
B_KR_COLS = B_ROPE
B_G_COLS = B_WIDTH
IN_COLS = A_Q_COLS + A_K_COLS + A_V_COLS + A_G_COLS + B_CQ_COLS + B_CKV_COLS + B_KR_COLS + B_G_COLS

kernel_name = "hybrid_swa_sink_mla_gated_block"

def rms_norm(x, w):
    xf = x.astype(jnp.float32)
    y = xf * lax.rsqrt(jnp.mean(xf * xf, axis=-1, keepdims=True) + EPS)
    return (y * w.astype(jnp.float32)).astype(x.dtype)

def rope_tables(positions, dim):
    inv_freq = 1.0 / (ROPE_THETA ** (jnp.arange(0, dim, 2, dtype=jnp.float32) / dim))
    ang = positions.astype(jnp.float32)[:, None] * inv_freq[None, :]
    return jnp.cos(ang), jnp.sin(ang)

def apply_rope(t, cos, sin):
    half = t.shape[-1] // 2
    t1, t2 = t[..., :half], t[..., half:]
    c = cos[None, :, None, :].astype(t.dtype)
    s = sin[None, :, None, :].astype(t.dtype)
    return jnp.concatenate([t1 * c - t2 * s, t2 * c + t1 * s], axis=-1)

def split_columns(h):
    sizes = [A_Q_COLS, A_K_COLS, A_V_COLS, A_G_COLS, B_CQ_COLS, B_CKV_COLS, B_KR_COLS, B_G_COLS]
    offs = [int(o) for o in np.cumsum(sizes)[:-1]]
    return jnp.split(h, offs, axis=-1)

def swa_sink_attention(q, k, v, sinks):
    bsz, seq = q.shape[0], q.shape[1]
    n_chunks = seq // CHUNK
    groups = A_HEADS // A_KV_HEADS
    qc = q.reshape(bsz, n_chunks, CHUNK, A_KV_HEADS, groups, A_HEAD_DIM)

    def band(t):
        tc = t.reshape(bsz, n_chunks, CHUNK, A_KV_HEADS, A_HEAD_DIM)
        shifted = [jnp.pad(tc, ((0, 0), (j, 0), (0, 0), (0, 0), (0, 0)))[:, :n_chunks]
                   for j in range(WINDOW_CHUNKS - 1, -1, -1)]
        return jnp.concatenate(shifted, axis=2)

    kb, vb = band(k), band(v)
    scale = A_HEAD_DIM ** -0.5
    scores = jnp.einsum('bcqhgd,bckhd->bhgcqk', qc, kb).astype(jnp.float32) * scale
    chunk_idx = jnp.arange(n_chunks)[:, None]
    back = (WINDOW_CHUNKS - 1) - jnp.arange(WINDOW_CHUNKS * CHUNK)[None, :] // CHUNK
    valid = (chunk_idx - back) >= 0
    scores = jnp.where(valid[None, None, None, :, None, :], scores, MASK_VALUE)
    sink = jnp.broadcast_to(
        sinks.astype(jnp.float32).reshape(A_KV_HEADS, groups)[None, :, :, None, None, None],
        scores.shape[:-1] + (1,))
    probs = jax.nn.softmax(jnp.concatenate([scores, sink], axis=-1), axis=-1)[..., :-1]
    out = jnp.einsum('bhgcqk,bckhd->bcqhgd', probs.astype(v.dtype), vb)
    return out.reshape(bsz, seq, A_WIDTH)

def mla_attention(q_nope, q_rope, k_nope, k_rope, v):
    bsz, seq = q_nope.shape[0], q_nope.shape[1]
    n_blocks = seq // Q_BLOCK
    scale = (B_NOPE + B_ROPE) ** -0.5
    k_chunk = jnp.arange(seq) // CHUNK

    def to_blocks(t):
        return jnp.moveaxis(t.reshape((bsz, n_blocks, Q_BLOCK) + t.shape[2:]), 1, 0)

    def one_block(args):
        qn, qr, blk = args
        s = (jnp.einsum('bqhd,bkhd->bhqk', qn, k_nope)
             + jnp.einsum('bqhd,bkd->bhqk', qr, k_rope)).astype(jnp.float32) * scale
        q_chunk = (blk * Q_BLOCK + jnp.arange(Q_BLOCK)) // CHUNK
        allowed = k_chunk[None, :] <= q_chunk[:, None]
        s = jnp.where(allowed[None, None], s, MASK_VALUE)
        p = jax.nn.softmax(s, axis=-1)
        return jnp.einsum('bhqk,bkhd->bqhd', p.astype(v.dtype), v)

    out = lax.map(one_block, (to_blocks(q_nope), to_blocks(q_rope), jnp.arange(n_blocks)))
    out = jnp.moveaxis(out, 0, 1)
    return out.reshape(bsz, seq, B_WIDTH)

def setup_inputs(seed: int = 0) -> dict:
    key = jax.random.key(seed)
    ks = jax.random.split(key, 10)
    f32 = jnp.float32
    x = jax.random.normal(ks[0], (BATCH, SEQ, D_MODEL), f32)
    norm_in_w = 1.0 + 0.02 * jax.random.normal(ks[1], (D_MODEL,), f32)
    w_in = jax.random.normal(ks[2], (D_MODEL, IN_COLS), f32) * D_MODEL ** -0.5
    sinks_a = jax.random.normal(ks[3], (A_HEADS,), f32)
    q_a_norm_w = 1.0 + 0.02 * jax.random.normal(ks[4], (B_Q_LORA,), f32)
    w_q_b = jax.random.normal(ks[5], (B_Q_LORA, B_HEADS * (B_NOPE + B_ROPE)), f32) * B_Q_LORA ** -0.5
    kv_a_norm_w = 1.0 + 0.02 * jax.random.normal(ks[6], (B_KV_LORA,), f32)
    w_kv_b = jax.random.normal(ks[7], (B_KV_LORA, B_HEADS * (B_NOPE + B_V)), f32) * B_KV_LORA ** -0.5
    w_out = jax.random.normal(ks[8], (MIX_WIDTH, D_MODEL), f32) * MIX_WIDTH ** -0.5
    final_norm_w = 1.0 + 0.02 * jax.random.normal(ks[9], (D_MODEL,), f32)
    return {"x": x, "norm_in_w": norm_in_w, "w_in": w_in, "sinks_a": sinks_a,
            "q_a_norm_w": q_a_norm_w, "w_q_b": w_q_b, "kv_a_norm_w": kv_a_norm_w,
            "w_kv_b": w_kv_b, "w_out": w_out, "final_norm_w": final_norm_w}

def reference(x, norm_in_w, w_in, sinks_a, q_a_norm_w, w_q_b, kv_a_norm_w, w_kv_b, w_out, final_norm_w):
    bsz, seq = x.shape[0], x.shape[1]
    positions = jnp.arange(seq, dtype=jnp.int32)
    cos_a, sin_a = rope_tables(positions, A_HEAD_DIM)
    cos_b, sin_b = rope_tables(positions, B_ROPE)

    for _ in range(DEPTH):
        h = rms_norm(x, norm_in_w)
        proj = jnp.einsum('bsd,dc->bsc', h, w_in)
        a_q, a_k, a_v, a_g, b_cq, b_ckv, b_kr, b_g = split_columns(proj)

        qa = apply_rope(a_q.reshape(bsz, seq, A_HEADS, A_HEAD_DIM), cos_a, sin_a)
        ka = apply_rope(a_k.reshape(bsz, seq, A_KV_HEADS, A_HEAD_DIM), cos_a, sin_a)
        va = a_v.reshape(bsz, seq, A_KV_HEADS, A_HEAD_DIM)
        out_a = swa_sink_attention(qa, ka, va, sinks_a) * jax.nn.silu(a_g)

        qb = jnp.einsum('bsr,rc->bsc', rms_norm(b_cq, q_a_norm_w), w_q_b)
        qb = qb.reshape(bsz, seq, B_HEADS, B_NOPE + B_ROPE)
        qb_nope = qb[..., :B_NOPE]
        qb_rope = apply_rope(qb[..., B_NOPE:], cos_b, sin_b)
        kvb = jnp.einsum('bsr,rc->bsc', rms_norm(b_ckv, kv_a_norm_w), w_kv_b)
        kvb = kvb.reshape(bsz, seq, B_HEADS, B_NOPE + B_V)
        kb_nope, vb = kvb[..., :B_NOPE], kvb[..., B_NOPE:]
        kb_rope = apply_rope(b_kr[:, :, None, :], cos_b, sin_b)[:, :, 0, :]
        out_b = mla_attention(qb_nope, qb_rope, kb_nope, kb_rope, vb) * jax.nn.silu(b_g)

        mixed = jnp.concatenate([out_a, out_b], axis=-1)
        x = x + jnp.einsum('bsc,cd->bsd', mixed, w_out)

    return rms_norm(x, final_norm_w)


_drawn_inputs = setup_inputs


def setup_inputs(seed=0):
    import zlib

    import numpy as np

    out = dict(_drawn_inputs(seed))
    spreads = {}
    factors = {'norm_in_w': 8.0,
     'sinks_a': 8.0,
     'q_a_norm_w': 8.0,
     'kv_a_norm_w': 8.0,
     'final_norm_w': 2.786}
    for name, (base, spread) in spreads.items():
        noise = np.random.default_rng([zlib.crc32(name.encode()), seed]).standard_normal(out[name].shape)
        drawn = base * np.exp(spread * noise) if base else spread * noise
        out[name] = __import__('jax').numpy.asarray(drawn.astype(out[name].dtype))
    for name, factor in factors.items():
        out[name] = (out[name] * factor).astype(out[name].dtype)
    return out
```

```python
from contextlib import ExitStack

import concourse.bass as bass
import numpy as np
from concourse import mybir

ALU = mybir.AluOpType
ACT = mybir.ActivationFunctionType
AX = mybir.AxisListType
F32 = mybir.dt.float32
F32R = mybir.dt.float32r
BF16 = mybir.dt.bfloat16

P = 128
D_MODEL, SEQ = 2048, 512
CHUNK = 64
EPS = 1e-6
MASK_VALUE = -1e30
A_HEADS, A_KV_HEADS, A_DIM = 16, 2, 64
B_HEADS, B_NOPE, B_ROPE, B_V = 8, 128, 64, 128
Q_LORA, KV_LORA = 512, 256
A_SCALE = A_DIM ** -0.5
B_SCALE = (B_NOPE + B_ROPE) ** -0.5
K_IN = D_MODEL // P
TOK = SEQ // P
A_TILES = A_HEADS * A_DIM // P
B_TILES = B_HEADS * B_V // P
MIX_TILES = A_TILES + B_TILES
CQ_T, CKV_T = Q_LORA // P, KV_LORA // P

CE = 1024
KV0 = 0
CQ0 = KV0 + 8
KR0 = CQ0 + 8
QA0 = KR0 + 2
GT0 = QA0 + 16
PB0 = GT0 + 32
WO0 = PB0 + 16
CHUNKS = WO0 + 32
RAW, HL = 2, 4
AHEAD = 3

T_CQ, T_KR, T_QA, T_GT = 4, 8, 9, 17
T_PB = T_GT + 16
PB_TILES = 7

A_UNITS = 8
AT_SCORES = {3: 0, 4: 1, 6: 2, 7: 3, 8: 4, 10: 5, 11: 6, 12: 7}
AT_TRANSPOSE = {5: 0, 6: 1, 8: 2, 9: 3, 10: 4, 12: 5, 13: 6, 14: 7}
AT_PV = {7: 0, 10: 1, 13: 2, 15: 3}


def build(nc, w_stream, x_t, x_nat, gains, final_w, tables, out):
    with ExitStack() as ctx:
        def sem(name):
            return ctx.enter_context(nc.semaphore(name))

        def bank(name):
            return ctx.enter_context(nc.psum_tensor(name, [P, 512], F32))

        base = (nc.sbuf_base + 31) // 32 * 32
        place = [base]

        def at(name, shape, dt, offset):
            return nc.alloc_sbuf_tensor_at(name, shape, dt, offset=offset)

        def region(nbytes):
            start = place[0]
            place[0] += (nbytes + 31) // 32 * 32
            return start

        r_x = region(2 * K_IN * SEQ * 4)
        x_hi = at("x_hi", [P, K_IN, SEQ], F32R, r_x)
        x_lo = at("x_lo", [P, K_IN, SEQ], F32R, r_x + K_IN * SEQ * 4)
        KB = 1024
        ma_hi = at("ma_hi", [P, A_TILES, SEQ], F32R, r_x)
        ma_lo = at("ma_lo", [P, A_TILES, SEQ], F32R, r_x + 16 * KB)
        cqs_hi = at("cqs_hi", [P, CQ_T, SEQ], F32R, r_x + 32 * KB)
        cqs_lo = at("cqs_lo", [P, CQ_T, SEQ], F32R, r_x + 40 * KB)
        ptb_hi = at("ptb_hi", [P, TOK, SEQ], F32R, r_x + 48 * KB)
        ptb_lo = at("ptb_lo", [P, TOK, SEQ], F32R, r_x + 56 * KB)
        mb_hi = at("mb_hi", [P, B_TILES, SEQ], F32R, r_x + 32 * KB)
        mb_lo = at("mb_lo", [P, B_TILES, SEQ], F32R, r_x + 48 * KB)

        r_mixed = region(MIX_TILES * SEQ * 4)
        mixed = at("mixed", [P, MIX_TILES, SEQ], F32, r_mixed)

        w_raw = at("w_raw", [P, RAW, CE], F32, region(RAW * CE * 4))
        w_hi = at("w_hi", [P, HL, CE], F32R, region(HL * CE * 4))
        w_lo = at("w_lo", [P, HL, CE], F32R, region(HL * CE * 4))

        gain = at("gain", [P, 38], F32, region(38 * 4))
        g_in, g_q, g_kv, sinks = gain[:, 0:16], gain[:, 16:20], gain[:, 20:22], gain[:, 22:38]
        neg_sinks = at("neg_sinks", [P, A_HEADS], F32, region(64))
        eps = at("eps", [P, 1], F32, region(4))
        ident = at("ident", [P, P], F32, region(512))
        ones = at("ones", [P, P], F32, region(512))
        ident_bf = at("ident_bf", [P, P], BF16, region(256))
        mask_bf = at("mask_bf", [P, 2, 2, CHUNK], BF16, region(512))
        st_a = at("st_a", [P, 2, 6, 2], F32, region(96))
        st_b = at("st_b", [P, 4, 4], F32, region(64))
        sumsq = at("sumsq", [P, TOK, 4], F32, region(64))
        fin = at("fin", [P, TOK, 3], F32, region(48))
        rstd = at("rstd", [P, SEQ], F32, region(2048))
        r_rot = region(4096)
        cos_r = at("cos_r", [P, SEQ], F32, r_rot)
        sin_r = at("sin_r", [P, SEQ], F32, r_rot + 2048)
        gate_tmp = at("gate_tmp", [P, 2, SEQ], F32, r_rot)
        cos_b = at("cos_b", [P, SEQ], F32, r_rot)
        sin_b = at("sin_b", [P, SEQ], F32, r_rot + 2048)
        r_ckv = region(8192)
        ckv_hi = at("ckv_hi", [P, CKV_T, SEQ], F32R, r_ckv)
        ckv_lo = at("ckv_lo", [P, CKV_T, SEQ], F32R, r_ckv + 4096)
        fw = at("fw", [P, D_MODEL], F32, r_ckv)
        cq = at("cq", [P, CQ_T, SEQ], F32, region(8192))
        kr_hi = at("kr_hi", [P, SEQ], F32R, region(2048))
        kr_lo = at("kr_lo", [P, SEQ], F32R, region(2048))
        r_tmp = region(6144)
        t1 = at("t1", [P, SEQ], F32, r_tmp)
        t2 = at("t2", [P, SEQ], F32, r_tmp + 2048)
        t3 = at("t3", [P, SEQ], F32, r_tmp + 4096)
        r4 = region(36 * KB)
        xs = at("xs", [P, 2, CE], F32, r4)
        sq = at("sq", [P, 2, CE], F32, r4 + 8 * KB)
        acc = at("acc", [P, CE], F32, r4 + 16 * KB)
        ckv = at("ckv", [P, CKV_T, SEQ], F32, r4 + 20 * KB)
        v_t = at("v_t", [P, SEQ], F32, r4 + 24 * KB)
        qs = at("qs", [P, 2, 2, SEQ], F32R, r4)
        ks_hi = at("ks_hi", [P, SEQ], F32R, r4 + 8 * KB)
        ks_lo = at("ks_lo", [P, SEQ], F32R, r4 + 10 * KB)
        va_hi = at("va_hi", [P, TOK, 2, P], F32R, r4 + 12 * KB)
        va_lo = at("va_lo", [P, TOK, 2, P], F32R, r4 + 16 * KB)
        pa = at("pa", [P, 2, 2, 4 * CHUNK], F32, r4 + 20 * KB)
        pta_hi = at("pta_hi", [P, 2, 384], F32R, r4 + 24 * KB)
        pta_lo = at("pta_lo", [P, 2, 384], F32R, r4 + 27 * KB)
        k_dup = at("k_dup", [P, A_KV_HEADS, SEQ], F32, r4 + 30 * KB)
        v_f = at("v_f", [P, TOK, P], F32, r4 + 34 * KB)
        qn_hi = at("qn_hi", [P, 2, SEQ], F32R, r4)
        qn_lo = at("qn_lo", [P, 2, SEQ], F32R, r4 + 4 * KB)
        kn_hi = at("kn_hi", [P, 2, SEQ], F32R, r4 + 8 * KB)
        kn_lo = at("kn_lo", [P, 2, SEQ], F32R, r4 + 12 * KB)
        qr = at("qr", [P, 2, SEQ], F32R, r4 + 16 * KB)
        vb_hi = at("vb_hi", [P, TOK, 2 * P], F32R, r4 + 20 * KB)
        vb_lo = at("vb_lo", [P, TOK, 2 * P], F32R, r4 + 24 * KB)
        pb = at("pb", [P, 4, SEQ], F32, r4 + 28 * KB)
        y = at("y", [P, TOK, D_MODEL], F32, r4)
        junk = at("junk", [P, SEQ], F32, r4 + 32 * KB)
        assert place[0] <= nc.sbuf_usable_end, place[0]

        B = [bank(f"bank{i}") for i in range(8)]

        w_landed = [sem(f"w_landed{i}") for i in range(RAW)]
        w_hi_ready, w_lo_ready, w_used = sem("w_hi_ready"), sem("w_lo_ready"), sem("w_used")
        x_landed = [sem("x_landed0"), sem("x_landed1")]
        x_hi_ready, x_lo_ready, x_squared, x_summed = sem("x_hi_ready"), sem("x_lo_ready"), sem("x_squared"), sem("x_summed")
        gains_landed, tables_landed, rot_landed, y_landed = sem("gains_landed"), sem("tables_landed"), sem("rot_landed"), sem("y_landed")
        consts_set = sem("consts_set")
        norm_sum, norm_total, norm_root, norm_recip = sem("norm_sum"), sem("norm_total"), sem("norm_root"), sem("norm_recip")
        proj_done, proj_evac = sem("proj_done"), sem("proj_evac")
        rot_terms, rotated, lat_scaled, lat_hi, lat_lo = sem("rot_terms"), sem("rotated"), sem("lat_scaled"), sem("lat_hi"), sem("lat_lo")
        v_turned, v_kept, squares = sem("v_turned"), sem("v_kept"), sem("squares")
        a_zeroed, a_split_hi, a_split_lo = sem("a_zeroed"), sem("a_split_hi"), sem("a_split_lo")
        a_scores, a_max, a_shift, a_exp, a_recip, a_probs = sem("a_scores"), sem("a_max"), sem("a_shift"), sem("a_exp"), sem("a_recip"), sem("a_probs")
        a_turned, a_pt_hi, a_pt_lo, a_pv, a_out = sem("a_turned"), sem("a_pt_hi"), sem("a_pt_lo"), sem("a_pv"), sem("a_out")
        gate_silu, gated = sem("gate_silu"), sem("gated")
        b_hi, b_rot, b_lo = sem("b_hi"), sem("b_rot"), sem("b_lo")
        b_scores, b_max, b_shift, b_exp, b_recip, b_probs = sem("b_scores"), sem("b_max"), sem("b_shift"), sem("b_exp"), sem("b_recip"), sem("b_probs")
        b_turned, b_pt_hi, b_pt_lo, b_pv, b_out = sem("b_turned"), sem("b_pt_hi"), sem("b_pt_lo"), sem("b_pv"), sem("b_out")
        m_hi, m_lo = sem("m_hi"), sem("m_lo")
        o_done, o_evac, o_squared, o_sum, o_root, o_recip, o_scaled, stored = (sem("o_done"), sem("o_evac"), sem("o_squared"), sem("o_sum"), sem("o_root"), sem("o_recip"), sem("o_scaled"), sem("stored"))

        block = ctx.enter_context(nc.Block())

        @block.sync
        def _(sp):
            for j in range(8):
                if j >= 2:
                    sp.wait_ge(x_lo_ready, j - 1)
                    sp.wait_ge(x_squared, j - 1)
                sp.dma_start(xs[:, j % 2, :], x_t[j, :, :]).then_inc(x_landed[j % 2], 16)
                if j >= RAW:
                    sp.wait_ge(w_lo_ready, j - 1)
                sp.dma_start(w_raw[:, j % RAW, :], w_stream[j, :, :]).then_inc(w_landed[j % RAW], 16)
            with sp.Fori(0, (CHUNKS - 8) // RAW) as i:
                for s in range(RAW):
                    sp.wait_ge(w_lo_ready, RAW * i + (7 + s))
                    sp.dma_start(w_raw[:, s, :], w_stream[bass.ds(RAW * i + (8 + s), 1), :, :].rearrange("a p c -> (a p) c"))\
                        .then_inc(w_landed[s], 16)
            for t in range(TOK):
                for h in range(2):
                    sp.wait_ge(o_scaled, 2 * t + h + 1)
                    sp.dma_start(out[0, P * t:P * t + P, CE * h:CE * h + CE], y[:, t, CE * h:CE * h + CE]).then_inc(stored, 16)
            sp.wait_ge(stored, 16 * 2 * TOK)

        @block.gpsimd
        def _(pool):
            def low_part(c, s):
                pool.wait_ge(w_hi_ready, c + 1)
                pool.tensor_tensor(w_lo[:, s % HL, :], w_raw[:, s % RAW, :], w_hi[:, s % HL, :].bitcast(F32), ALU.subtract)\
                    .then_inc(w_lo_ready, 1)

            with pool.Fori(0, CHUNKS // HL) as i:
                for s in range(HL):
                    low_part(HL * i + s, s)
            for c in range(CHUNKS // HL * HL, CHUNKS):
                low_part(c, c)

        @block.scalar
        def _(act):
            def high_part(c, s):
                act.wait_ge(w_landed[s % RAW], 8 * (c - s % RAW) + 16)
                if not isinstance(c, int) or c >= HL:
                    act.wait_ge(w_used, c - (HL - 1))
                act.activation(w_hi[:, s % HL, :], w_raw[:, s % RAW, :], ACT.Copy).then_inc(w_hi_ready, 1)

            def x_parts(j):
                act.wait_ge(x_landed[j % 2], 16 * (j // 2 + 1))
                for h in range(2):
                    k = 2 * j + h
                    ins = act.activation(x_hi[:, k, :], xs[:, j % 2, SEQ * h:SEQ * h + SEQ], ACT.Copy, scale=g_in[:, k:k + 1])
                ins.then_inc(x_hi_ready, 1)
                if j >= 3:
                    act.wait_ge(x_summed, j - 2)
                act.activation(acc[:, :] if j == 0 else sq[:, j % 2, :], xs[:, j % 2, :], ACT.Square).then_inc(x_squared, 1)

            act.dma_start(gain[:, :], gains[:, :]).then_inc(gains_landed, 16)
            act.dma_start(ident[:, :], tables[:, 0:P]).then_inc(tables_landed, 16)
            act.dma_start(cos_r[:, :], tables[:, P:P + SEQ]).then_inc(tables_landed, 16)
            act.dma_start(sin_r[:, :], tables[:, P + SEQ:P + 2 * SEQ]).then_inc(tables_landed, 16)
            act.sem_inc(a_exp, 2)
            act.sem_inc(b_exp, 2)
            act.wait_ge(gains_landed, 16)
            high_part(0, 0)
            x_parts(0)
            high_part(1, 1)
            x_parts(1)
            high_part(2, 2)

            def root(n, total, width):
                act.wait_ge(norm_total, n)
                act.wait_ge(consts_set, 1)
                act.activation(t2[:, :], total, ACT.Sqrt, bias=eps[:, :], scale=1.0 / width).then_inc(norm_root, 1)

            for c in range(GT0):
                if c + 2 < 8:
                    x_parts(c + 2)
                high_part(c + AHEAD, c + AHEAD)
                if c == 8:
                    root(1, B[7][:, :], D_MODEL)
                if c == QA0:
                    act.wait_ge(proj_evac, T_KR)
                    act.activation(sq[:, 0, :], ckv[:, :, :].rearrange("p a b -> p (a b)"), ACT.Square).then_inc(squares, 1)
                    act.activation(sq[:, 1, :], cq[:, 0:2, :].rearrange("p a b -> p (a b)"), ACT.Square).then_inc(squares, 1)
                    act.wait_ge(norm_sum, 1)
                    act.activation(acc[:, :], cq[:, 2:4, :].rearrange("p a b -> p (a b)"), ACT.Square).then_inc(squares, 1)
                    act.wait_ge(rotated, 2)
                    act.activation(kr_hi[:, :], t3[:, :], ACT.Copy).then_inc(lat_hi, 1)
                if c == QA0 + 8:
                    act.wait_ge(rotated, 6)
                    root(2, B[1][:, :], KV_LORA)
                    act.wait_ge(norm_recip, 2)
                    root(3, B[2][:, :], Q_LORA)
                    act.wait_ge(lat_scaled, 1)
                    act.activation(ckv_hi[:, :, :], ckv[:, :, :], ACT.Copy).then_inc(lat_hi, 1)

            def a_split(t):
                act.wait_ge(a_pv, 4 * t + 1)
                act.activation(qs[0:64, :, 0, :], mixed[0:64, bass.ds(2 * t, 2), :], ACT.Copy)
                act.activation(qs[64:128, :, 1, :], mixed[64:128, bass.ds(2 * t, 2), :], ACT.Copy).then_inc(a_split_hi, 1)
                g = t // 2
                act.activation(ks_hi[:, :], k_dup[:, bass.ds(g, 1), :].rearrange("p a b -> p (a b)"), ACT.Copy)
                act.activation(va_hi[:, :, 0, 0:64], v_f[:, :, bass.ds(64 * g, 64)], ACT.Copy)
                act.activation(va_hi[:, :, 1, 64:128], v_f[:, :, bass.ds(64 * g, 64)], ACT.Copy).then_inc(a_split_hi, 1)

            def a_exps(t, u):
                i, slot = u // 2, u % 2
                w = 2 * CHUNK if i == 0 else 3 * CHUNK
                act.wait_ge(a_turned, A_UNITS * t + u + 1)
                act.wait_ge(a_shift, A_UNITS * t + u + 1)
                st = st_a[:, slot, :, :]
                for e in range(2):
                    act.activation(pa[:, slot, e, 4 * CHUNK - w:], B[4 + slot][:, 192 * e + 192 - w:192 * e + 192], ACT.Exp,
                                   bias=st[:, 1, e:e + 1], scale=A_SCALE, accum_out=st[:, 3, e:e + 1])
                act.activation(st[:, 4, :], st[:, 2, :], ACT.Exp).then_inc(a_exp, 1)

            def a_pt_high(t, u):
                i, m = u // 2, u % 2
                act.wait_ge(a_turned, A_UNITS * t + u + 3)
                if m == 0:
                    act.wait_ge(a_pv, TOK * t + i + 1)
                ins = act.activation(pta_hi[:, m, 0:256], B[6][:, 0:256], ACT.Copy)
                if i > 0:
                    ins = act.activation(pta_hi[:, m, 256:384].rearrange("p (a b) -> p a b", a=2),
                                   B[6][:, 256:512].rearrange("p (a b) -> p a b", a=2)[:, :, 0:64], ACT.Copy)
                ins.then_inc(a_pt_hi, 1)

            act.wait_ge(a_zeroed, 1)
            act.wait_ge(v_kept, 1)
            act.wait_ge(proj_evac, T_GT)
            with act.Fori(0, 4) as t:
                for hf in range(16):
                    if hf % 2 == 0:
                        high_part(8 * t + (GT0 + AHEAD + hf // 2), GT0 + AHEAD + hf // 2)
                    if hf == 0:
                        a_split(t)
                    if hf in AT_TRANSPOSE:
                        a_pt_high(t, AT_TRANSPOSE[hf])
                    if hf in AT_SCORES:
                        a_exps(t, AT_SCORES[hf])
                for ct in range(4):
                    act.wait_ge(proj_evac, 4 * t + (T_GT + ct + 1))
                    dst = gate_tmp[:, ct, :] if ct < 2 else mixed[:, bass.ds(2 * t + (A_TILES + ct - 2), 1), :].rearrange("p a b -> p (a b)")
                    act.activation(dst, dst, ACT.Silu).then_inc(gate_silu, 1)

            act.wait_ge(gated, 8)
            act.dma_start(cos_b[:, :], tables[:, P:P + SEQ]).then_inc(rot_landed, 16)
            act.dma_start(sin_b[:, :], tables[:, P + SEQ:P + 2 * SEQ]).then_inc(rot_landed, 16)
            act.wait_ge(w_used, PB0)
            for k in range(CQ_T):
                act.activation(cqs_hi[:, k, :], cq[:, k, :], ACT.Copy).then_inc(lat_hi, 1)
            with act.Fori(0, 4) as p:
                high_part(4 * p + (PB0 + AHEAD), PB0 + AHEAD)

                def tile_high(n, dst, src):
                    act.wait_ge(proj_done, PB_TILES * p + (T_PB + n + 1))
                    act.activation(dst, src, ACT.Copy).then_inc(b_hi, 1)

                tile_high(0, kn_hi[:, 0, :], B[0][:, :])
                tile_high(1, vb_hi[:, 0:2, :], B[1][:, :].rearrange("p (a b) -> p a b", a=2))
                tile_high(2, vb_hi[:, 2:4, :], B[2][:, :].rearrange("p (a b) -> p a b", a=2))
                tile_high(3, kn_hi[:, 1, :], B[3][:, :])
                tile_high(5, qn_hi[:, 0, :], B[1][:, :])
                act.wait_ge(b_rot, p + 1)
                act.activation(qr[0:64, 0, :], t3[0:64, :], ACT.Copy)
                act.activation(qr[64:128, 1, :], t3[64:128, :], ACT.Copy).then_inc(b_hi, 1)
                tile_high(6, qn_hi[:, 1, :], B[2][:, :])

                def b_expo(u):
                    n = P * (u % 4 + 1)
                    act.wait_ge(b_turned, 8 * p + u + 1)
                    act.wait_ge(b_shift, 8 * p + u + 1)
                    act.activation(pb[:, u % 4, 0:n], B[4 + u % 2][:, 0:n], ACT.Exp, bias=st_b[:, u % 4, 1:2], scale=B_SCALE,
                                   accum_out=st_b[:, u % 4, 2:3]).then_inc(b_exp, 1)

                def b_pt_high(u):
                    i = u % 4
                    act.wait_ge(b_turned, 8 * p + u + 5)
                    if i == 0:
                        act.wait_ge(b_pv, 2 * p + u // 4 + 1)
                    act.activation(ptb_hi[:, 0:i + 1, P * i:P * i + P],
                                   B[(6, 3)[u % 2]][:, 0:P * (i + 1)].rearrange("p (a b) -> p a b", a=i + 1), ACT.Copy).then_inc(b_pt_hi, 1)

                for u in range(4):
                    b_expo(u)
                    if u > 0:
                        high_part(4 * p + (PB0 + AHEAD + u), PB0 + AHEAD + u)
                for u in range(4):
                    b_pt_high(u)
                    b_expo(4 + u)
                act.activation(ma_hi[:, bass.ds(2 * p, 2), :], mixed[:, bass.ds(2 * p, 2), :], ACT.Copy).then_inc(m_hi, 1)
                for u in range(4, 8):
                    b_pt_high(u)

            act.wait_ge(b_pv, 9)
            act.wait_ge(b_out, 9)
            act.dma_start(y[:, :, :], x_nat[0, :, :].rearrange("(t p) d -> p t d", p=P)).then_inc(y_landed, 16)
            act.dma_start(fw[:, :], final_w[:, :]).then_inc(y_landed, 16)
            for m in range(4):
                act.activation(mb_hi[:, 2 * m:2 * m + 2, :], mixed[:, A_TILES + 2 * m:A_TILES + 2 * m + 2, :], ACT.Copy).then_inc(m_hi, 1)

            def out_squares(n):
                for t in range(TOK):
                    act.wait_ge(o_evac, 4 * n + (t + 5))
                    ss = sumsq[:, t, bass.ds(n, 1)] if not isinstance(n, int) else sumsq[:, t, n:n + 1]
                    act.wait_ge(o_squared, 4 * n + (t + 1))
                    act.activation(junk[:, :], y[:, t, bass.ds(SEQ * n, SEQ)], ACT.Square, accum_out=ss).then_inc(o_squared, 1)

            act.sem_inc(o_squared, 1)
            with act.Fori(0, 3) as n:
                for s in range(8):
                    high_part(8 * n + (WO0 + AHEAD + s), WO0 + AHEAD + s)
                out_squares(n)
            for s in range(8 - AHEAD):
                high_part(WO0 + 24 + AHEAD + s, WO0 + 24 + AHEAD + s)
            out_squares(3)
            for t in range(TOK):
                act.wait_ge(o_sum, t + 1)
                act.activation(fin[:, t, 1:2], fin[:, t, 0:1], ACT.Sqrt, bias=eps[:, :], scale=1.0 / D_MODEL).then_inc(o_root, 1)

        @block.vector
        def _(dve):
            dve.memset(eps[:, :], EPS).then_inc(consts_set, 1)
            dve.memset(ones[:, :], 1.0).then_inc(consts_set, 1)
            dve.memset(mask_bf[:, :, :, :], 0.0).then_inc(consts_set, 1)
            dve.wait_ge(consts_set, 3)
            dve.memset(mask_bf[64:128, 0, :, :], MASK_VALUE)
            dve.memset(mask_bf[0:64, 1, :, :], MASK_VALUE).then_inc(consts_set, 1)
            dve.sem_inc(a_pt_lo, 1)
            dve.sem_inc(a_out, 1)
            dve.sem_inc(b_pt_lo, 2)
            dve.sem_inc(b_out, 1)
            dve.sem_inc(o_evac, 4)
            dve.wait_ge(gains_landed, 16)
            dve.tensor_scalar(neg_sinks[:, :], sinks, -1.0, None, ALU.mult).then_inc(consts_set, 1)
            dve.wait_ge(tables_landed, 48)
            dve.tensor_copy(ident_bf[:, :], ident[:, :]).then_inc(consts_set, 1)

            for j in range(8):
                dve.wait_ge(x_hi_ready, j + 1)
                for h in range(2):
                    k = 2 * j + h
                    ins = dve.scalar_tensor_tensor(out=x_lo[:, k, :], in0=xs[:, j % 2, SEQ * h:SEQ * h + SEQ], scalar=g_in[:, k:k + 1],
                                                   op0=ALU.mult, in1=x_hi[:, k, :].bitcast(F32), op1=ALU.subtract)
                ins.then_inc(x_lo_ready, 1)
                if j >= 1:
                    dve.wait_ge(x_squared, j + 1)
                    if j >= 2:
                        dve.wait_ge(x_summed, j - 1)
                    dve.tensor_tensor(acc[:, :], acc[:, :], sq[:, j % 2, :], ALU.add).then_inc(x_summed, 1)
            dve.wait_ge(x_summed, 7)
            dve.tensor_tensor(t1[:, :], acc[:, 0:SEQ], acc[:, SEQ:CE], ALU.add).then_inc(norm_sum, 1)
            dve.wait_ge(norm_root, 1)
            dve.reciprocal(rstd[:, :], t2[:, :]).then_inc(norm_recip, 1)
            dve.wait_ge(norm_recip, 1)
            dve.tensor_tensor(cos_r[:, :], cos_r[:, :], rstd[:, :], ALU.mult)
            dve.tensor_tensor(sin_r[:, :], sin_r[:, :], rstd[:, :], ALU.mult).then_inc(consts_set, 1)
            dve.wait_ge(consts_set, 7)

            def rotate_terms(src, cos, sin, count):
                dve.tensor_tensor(t1[:, :], src[:, :], cos[:, :], ALU.mult)
                for q in range(4):
                    o = q ^ 1
                    ins = dve.tensor_tensor(t2[32 * q:32 * q + 32, :], src[32 * o:32 * o + 32, :], sin[32 * q:32 * q + 32, :], ALU.mult)
                ins.then_inc(proj_evac, 1)
                dve.wait_ge(proj_evac, count)

            dve.wait_ge(proj_done, 1)
            rotate_terms(B[0], cos_r, sin_r, 1)
            for g in range(A_KV_HEADS):
                for h in range(2):
                    ins = dve.tensor_tensor(k_dup[64 * h:64 * h + 64, g, :], t1[64 * g:64 * g + 64, :], t2[64 * g:64 * g + 64, :], ALU.add)
            ins.then_inc(rotated, 1)
            dve.wait_ge(proj_done, 2)
            dve.tensor_tensor(v_t[:, :], B[1][:, :], rstd[:, :], ALU.mult).then_inc(proj_evac, 1)
            for j in range(CKV_T):
                dve.wait_ge(proj_done, 3 + j)
                dve.tensor_tensor(ckv[:, j, :], B[2 + j][:, :], rstd[:, :], ALU.mult).then_inc(proj_evac, 1)
            for j in range(CQ_T):
                dve.wait_ge(proj_done, T_CQ + 1 + j)
                dve.tensor_tensor(cq[:, j, :], B[4 + j][:, :], rstd[:, :], ALU.mult).then_inc(proj_evac, 1)
            dve.wait_ge(proj_done, T_KR + 1)
            dve.wait_ge(rotated, 1)
            rotate_terms(B[0], cos_r, sin_r, T_KR + 1)
            dve.wait_ge(norm_root, 1)
            dve.tensor_tensor(t3[:, :], t1[:, :], t2[:, :], ALU.add).then_inc(rotated, 1)
            dve.wait_ge(lat_hi, 1)
            dve.tensor_tensor(kr_lo[:, :], t3[:, :], kr_hi[:, :].bitcast(F32), ALU.subtract).then_inc(lat_lo, 1)
            dve.wait_ge(squares, 3)
            dve.wait_ge(lat_lo, 1)
            dve.tensor_tensor(t3[:, :], sq[:, 0, 0:SEQ], sq[:, 0, SEQ:CE], ALU.add).then_inc(norm_sum, 1)
            dve.tensor_tensor(sq[:, 1, :], sq[:, 1, :], acc[:, :], ALU.add).then_inc(squares, 1)
            dve.wait_ge(squares, 4)
            dve.tensor_tensor(sq[:, 0, 0:SEQ], sq[:, 1, 0:SEQ], sq[:, 1, SEQ:CE], ALU.add).then_inc(norm_sum, 1)

            def a_query(m):
                dve.wait_ge(proj_done, T_QA + 1 + m)
                dve.wait_ge(rotated, 2 + m)
                rotate_terms(B[(4 + m) % 8], cos_r, sin_r, T_QA + 1 + m)
                dve.tensor_tensor(mixed[:, m, :], t1[:, :], t2[:, :], ALU.add).then_inc(rotated, 1)

            for m in range(4):
                a_query(m)
            dve.wait_ge(norm_root, 2)
            dve.reciprocal(t3[:, :], t2[:, :]).then_inc(norm_recip, 1)
            dve.wait_ge(norm_recip, 2)
            for j in range(CKV_T):
                ins = dve.scalar_tensor_tensor(out=ckv[:, j, :], in0=ckv[:, j, :], scalar=g_kv[:, j:j + 1], op0=ALU.mult,
                                               in1=t3[:, :], op1=ALU.mult)
            ins.then_inc(lat_scaled, 1)
            dve.wait_ge(norm_root, 3)
            dve.wait_ge(lat_scaled, 1)
            dve.reciprocal(t3[:, :], t2[:, :]).then_inc(norm_recip, 1)
            dve.wait_ge(norm_recip, 3)
            for j in range(CQ_T):
                ins = dve.scalar_tensor_tensor(out=cq[:, j, :], in0=cq[:, j, :], scalar=g_q[:, j:j + 1], op0=ALU.mult,
                                               in1=t3[:, :], op1=ALU.mult)
            ins.then_inc(lat_scaled, 1)
            dve.wait_ge(lat_hi, 2)
            dve.tensor_tensor(ckv_lo[:, :, :], ckv[:, :, :], ckv_hi[:, :, :].bitcast(F32), ALU.subtract).then_inc(lat_lo, 1)
            dve.wait_ge(v_turned, 1)
            dve.tensor_copy(v_f[:, :, :], B[3][:, :].rearrange("p (a b) -> p a b", a=TOK)).then_inc(v_kept, 1)
            dve.wait_ge(norm_total, 3)
            dve.wait_ge(lat_lo, 2)
            dve.memset(va_hi[:, :, 0, 64:128].bitcast(F32), 0.0)
            dve.memset(va_hi[:, :, 1, 0:64].bitcast(F32), 0.0)
            dve.memset(va_lo[:, :, 0, 64:128].bitcast(F32), 0.0)
            dve.memset(va_lo[:, :, 1, 0:64].bitcast(F32), 0.0)
            dve.memset(pa[:, :, :, :], 0.0).then_inc(a_zeroed, 1)
            for m in range(4, 8):
                a_query(m)

            def a_maxima(t, u):
                i, m, slot = u // 2, u % 2, u % 2
                w = 2 * CHUNK if i == 0 else 3 * CHUNK
                st = st_a[:, slot, :, :]
                hd = bass.ds(4 * t + 2 * m, 2)
                dve.wait_ge(a_scores, A_UNITS * t + u + 1)
                dve.reduce_max(st[:, 0, :], B[4 + slot][:, 0:384].rearrange("p (a b) -> p a b", a=2)[:, :, 192 - w:192], AX.X).then_inc(a_max, 1)
                dve.wait_ge(a_max, 2 * (A_UNITS * t + u) + 1)
                dve.scalar_tensor_tensor(out=st[:, 1, :], in0=st[:, 0, :], scalar=-A_SCALE, op0=ALU.mult,
                                         in1=neg_sinks[:, hd], op1=ALU.min).then_inc(a_max, 1)
                dve.wait_ge(a_max, 2 * (A_UNITS * t + u) + 2)
                dve.tensor_tensor(st[:, 2, :], st[:, 1, :], sinks[:, hd], ALU.add).then_inc(a_shift, 1)

            def a_normalise(t, u):
                slot = u % 2
                st = st_a[:, slot, :, :]
                dve.wait_ge(a_exp, A_UNITS * t + u + 3)
                dve.tensor_tensor(st[:, 5, :], st[:, 3, :], st[:, 4, :], ALU.add).then_inc(a_recip, 1)
                dve.wait_ge(a_recip, 2 * (A_UNITS * t + u) + 1)
                dve.reciprocal(st[:, 5, :], st[:, 5, :]).then_inc(a_recip, 1)
                dve.wait_ge(a_recip, 2 * (A_UNITS * t + u) + 2)
                for e in range(2):
                    ins = dve.tensor_scalar(pa[:, slot, e, CHUNK:], pa[:, slot, e, CHUNK:], st[:, 5, e:e + 1], None, ALU.mult)
                ins.then_inc(a_probs, 1)

            def a_pt_low(t, u):
                i, m = u // 2, u % 2
                dve.wait_ge(a_pt_hi, A_UNITS * t + u + 1)
                ins = dve.tensor_tensor(pta_lo[:, m, 0:256], B[6][:, 0:256], pta_hi[:, m, 0:256].bitcast(F32), ALU.subtract)
                if i > 0:
                    ins = dve.tensor_tensor(pta_lo[:, m, 256:384].rearrange("p (a b) -> p a b", a=2),
                                            B[6][:, 256:512].rearrange("p (a b) -> p a b", a=2)[:, :, 0:64],
                                            pta_hi[:, m, 256:384].bitcast(F32).rearrange("p (a b) -> p a b", a=2), ALU.subtract)
                ins.then_inc(a_pt_lo, 1)

            dve.wait_ge(rotated, 10)
            with dve.Fori(0, 4) as t:
                dve.wait_ge(a_split_hi, 2 * t + 1)
                dve.tensor_tensor(qs[64:128, :, 0, :], mixed[0:64, bass.ds(2 * t, 2), :], qs[0:64, :, 0, :].bitcast(F32), ALU.subtract)
                dve.tensor_tensor(qs[0:64, :, 1, :], mixed[64:128, bass.ds(2 * t, 2), :], qs[64:128, :, 1, :].bitcast(F32), ALU.subtract)
                dve.wait_ge(a_split_hi, 2 * t + 2)
                g = t // 2
                dve.tensor_tensor(ks_lo[:, :], k_dup[:, bass.ds(g, 1), :].rearrange("p a b -> p (a b)"), ks_hi[:, :].bitcast(F32), ALU.subtract)
                for e in range(2):
                    ins = dve.tensor_tensor(va_lo[:, :, e, 64 * e:64 * e + 64], v_f[:, :, bass.ds(64 * g, 64)],
                                            va_hi[:, :, e, 64 * e:64 * e + 64].bitcast(F32), ALU.subtract)
                ins.then_inc(a_split_lo, 1)
                last = None
                for hf in range(16):
                    if last is not None:
                        a_normalise(t, last)
                        last = None
                    if hf in AT_SCORES:
                        a_maxima(t, AT_SCORES[hf])
                        last = AT_SCORES[hf]
                    if hf in AT_TRANSPOSE:
                        a_pt_low(t, AT_TRANSPOSE[hf])
                    if hf in AT_PV:
                        i = AT_PV[hf]
                        dve.wait_ge(a_pv, TOK * t + i + 2)
                        dve.tensor_scalar(mixed[:, bass.ds(2 * t, 2), P * i:P * i + P], B[7][:, 0:256].rearrange("p (a b) -> p a b", a=2),
                                          1.0, None, ALU.mult).then_inc(a_out, 1)
                for ct in range(4):
                    dve.wait_ge(proj_done, 4 * t + (T_GT + ct + 1))
                    dst = gate_tmp[:, ct, :] if ct < 2 else mixed[:, bass.ds(2 * t + (A_TILES + ct - 2), 1), :].rearrange("p a b -> p (a b)")
                    dve.tensor_tensor(dst, B[ct][:, :], rstd[:, :], ALU.mult).then_inc(proj_evac, 1)
                dve.wait_ge(a_out, TOK * t + 5)
                for ct in range(2):
                    dve.wait_ge(gate_silu, 4 * t + (ct + 1))
                    m = mixed[:, bass.ds(2 * t + ct, 1), :].rearrange("p a b -> p (a b)")
                    dve.tensor_tensor(m, m, gate_tmp[:, ct, :], ALU.mult).then_inc(gated, 1)
                dve.wait_ge(gated, 2 * t + 2)

            for k in range(CQ_T):
                dve.wait_ge(lat_hi, 3 + k)
                dve.tensor_tensor(cqs_lo[:, k, :], cq[:, k, :], cqs_hi[:, k, :].bitcast(F32), ALU.subtract).then_inc(lat_lo, 1)
            dve.wait_ge(rot_landed, 32)
            dve.wait_ge(gate_silu, 16)
            with dve.Fori(0, 4) as p:
                def tile_low(k, dst, src, hi):
                    dve.wait_ge(b_hi, PB_TILES * p + (k + 1))
                    dve.tensor_tensor(dst, src, hi.bitcast(F32), ALU.subtract).then_inc(proj_evac, 1)

                halves = "p (a b) -> p a b"
                tile_low(0, kn_lo[:, 0, :], B[0][:, :], kn_hi[:, 0, :])
                tile_low(1, vb_lo[:, 0:2, :], B[1][:, :].rearrange(halves, a=2), vb_hi[:, 0:2, :])
                tile_low(2, vb_lo[:, 2:4, :], B[2][:, :].rearrange(halves, a=2), vb_hi[:, 2:4, :])
                tile_low(3, kn_lo[:, 1, :], B[3][:, :], kn_hi[:, 1, :])
                dve.wait_ge(proj_done, PB_TILES * p + (T_PB + 5))
                rotate_terms(B[0], cos_b, sin_b, PB_TILES * p + (T_PB + 5))
                dve.tensor_tensor(t3[:, :], t1[:, :], t2[:, :], ALU.add).then_inc(b_rot, 1)
                dve.wait_ge(b_rot, p + 1)
                tile_low(4, qn_lo[:, 0, :], B[1][:, :], qn_hi[:, 0, :])
                dve.wait_ge(b_hi, PB_TILES * p + 6)
                dve.tensor_tensor(qr[64:128, 0, :], t3[0:64, :], qr[0:64, 0, :].bitcast(F32), ALU.subtract)
                dve.tensor_tensor(qr[0:64, 1, :], t3[64:128, :], qr[64:128, 1, :].bitcast(F32), ALU.subtract).then_inc(b_lo, 1)
                dve.wait_ge(b_lo, p + 1)
                tile_low(6, qn_lo[:, 1, :], B[2][:, :], qn_hi[:, 1, :])

                def b_maxima(u):
                    n = P * (u % 4 + 1)
                    dve.wait_ge(b_scores, 8 * p + u + 1)
                    dve.reduce_max(st_b[:, u % 4, 0:1], B[4 + u % 2][:, 0:n], AX.X).then_inc(b_max, 1)
                    dve.wait_ge(b_max, 8 * p + u + 1)
                    dve.tensor_scalar(st_b[:, u % 4, 1:2], st_b[:, u % 4, 0:1], -B_SCALE, None, ALU.mult).then_inc(b_shift, 1)

                def b_normalise(u):
                    n = P * (u % 4 + 1)
                    dve.wait_ge(b_exp, 8 * p + u + 3)
                    dve.reciprocal(st_b[:, u % 4, 3:4], st_b[:, u % 4, 2:3]).then_inc(b_recip, 1)
                    dve.wait_ge(b_recip, 8 * p + u + 1)
                    dve.tensor_scalar(pb[:, u % 4, 0:n], pb[:, u % 4, 0:n], st_b[:, u % 4, 3:4], None, ALU.mult).then_inc(b_probs, 1)

                def b_pt_low(u):
                    i = u % 4
                    dve.wait_ge(b_pt_hi, 8 * p + u + 1)
                    dve.tensor_tensor(ptb_lo[:, 0:i + 1, P * i:P * i + P],
                                      B[(6, 3)[u % 2]][:, 0:P * (i + 1)].rearrange("p (a b) -> p a b", a=i + 1),
                                      ptb_hi[:, 0:i + 1, P * i:P * i + P].bitcast(F32), ALU.subtract).then_inc(b_pt_lo, 1)

                def b_take(h):
                    dve.wait_ge(b_pv, 2 * p + h + 2)
                    m = mixed[:, bass.ds(2 * p + (A_TILES + h), 1), :].rearrange("p a b -> p (a b)")
                    dve.tensor_tensor(m, B[7][:, :], m, ALU.mult).then_inc(b_out, 1)

                for u in range(4):
                    b_maxima(u)
                    if u > 0:
                        b_normalise(u - 1)
                b_maxima(4)
                b_normalise(3)
                for u in range(4):
                    b_pt_low(u)
                    if u < 3:
                        b_maxima(5 + u)
                    b_normalise(4 + u)
                b_take(0)
                for u in range(4, 8):
                    b_pt_low(u)
                dve.wait_ge(m_hi, p + 1)
                dve.tensor_tensor(ma_lo[:, bass.ds(2 * p, 2), :], mixed[:, bass.ds(2 * p, 2), :],
                                  ma_hi[:, bass.ds(2 * p, 2), :].bitcast(F32), ALU.subtract).then_inc(m_lo, 1)
                b_take(1)

            dve.wait_ge(b_out, 9)
            for m in range(4):
                dve.wait_ge(m_hi, 5 + m)
                dve.tensor_tensor(mb_lo[:, 2 * m:2 * m + 2, :], mixed[:, A_TILES + 2 * m:A_TILES + 2 * m + 2, :],
                                  mb_hi[:, 2 * m:2 * m + 2, :].bitcast(F32), ALU.subtract).then_inc(m_lo, 1)
            dve.wait_ge(y_landed, 32)

            def residual(n):
                for t in range(TOK):
                    dve.wait_ge(o_done, 4 * n + (t + 1))
                    ys = y[:, t, bass.ds(SEQ * n, SEQ)]
                    dve.tensor_tensor(ys, B[t][:, :], ys, ALU.add).then_inc(o_evac, 1)

            with dve.Fori(0, 3) as n:
                residual(n)
            residual(3)
            for t in range(TOK):
                dve.wait_ge(o_squared, 12 + t + 2)
                dve.reduce_sum(fin[:, t, 0:1], sumsq[:, t, :], AX.X).then_inc(o_sum, 1)
                dve.wait_ge(o_root, t + 1)
                dve.reciprocal(fin[:, t, 2:3], fin[:, t, 1:2]).then_inc(o_recip, 1)
                dve.wait_ge(o_recip, t + 1)
                for h in range(2):
                    ys = y[:, t, CE * h:CE * h + CE]
                    dve.scalar_tensor_tensor(out=ys, in0=ys, scalar=fin[:, t, 2:3], op0=ALU.mult, in1=fw[:, CE * h:CE * h + CE], op1=ALU.mult)\
                        .then_inc(o_scaled, 1)

        @block.tensor
        def _(pe):
            def three(dst, ah, al, bh, bl, start, stop, frees_chunk=False):
                ins = pe.matmul(dst, ah, bh, start=start, stop=False)
                if frees_chunk:
                    ins.then_inc(w_used, 1)
                pe.matmul(dst, al, bh, start=False, stop=False)
                return pe.matmul(dst, ah, bl, start=False, stop=stop)

            def columns(s, banks, tiles, ks, frees_chunk, width=SEQ):
                for ct in tiles:
                    for n, k in enumerate(ks):
                        o = width * n + P * ct
                        ins = three(B[banks[ct]][:, :], w_hi[:, s % HL, o:o + P], w_lo[:, s % HL, o:o + P],
                                    x_hi[:, k, :], x_lo[:, k, :], k == 0, k == K_IN - 1, frees_chunk and ct == tiles[0] and n == 0)
                    if ks[-1] == K_IN - 1:
                        ins.then_inc(proj_done, 1)

            def group(c0, banks, free=None, with_x=False):
                for s in range(8):
                    pe.wait_ge(w_lo_ready, c0 + s + 1)
                    if with_x:
                        pe.wait_ge(x_lo_ready, s + 1)
                    for ct in range(4):
                        if s == 0 and free is not None:
                            pe.wait_ge(proj_evac, free + ct)
                        columns(c0 + s, banks, (ct,), (2 * s, 2 * s + 1), ct == 0 and c0 + s > 0)

            pe.sem_inc(a_turned, 2)
            pe.sem_inc(a_pv, 1)
            pe.sem_inc(b_turned, 4)
            pe.sem_inc(b_pv, 1)
            group(KV0, (0, 1, 2, 3), with_x=True)
            pe.wait_ge(consts_set, 2)
            pe.wait_ge(norm_sum, 1)
            pe.matmul(B[7][:, :], ones[:, :], t1[:, :], start=True, stop=True).then_inc(norm_total, 1)
            for s in range(8):
                pe.wait_ge(w_lo_ready, CQ0 + s + 1)
                for ct in range(4):
                    if s == 0 and ct == 3:
                        pe.wait_ge(norm_root, 1)
                    columns(CQ0 + s, (4, 5, 6, 7), (ct,), (2 * s, 2 * s + 1), ct == 0)
            pe.wait_ge(proj_evac, 1)
            for s in range(2):
                pe.wait_ge(w_lo_ready, KR0 + s + 1)
                columns(KR0 + s, (0,), (0,), tuple(range(8 * s, 8 * s + 8)), True, width=P)
            group(QA0, (4, 5, 6, 7), free=T_CQ + 1)
            pe.wait_ge(proj_evac, 4)
            pe.wait_ge(tables_landed, 48)
            for t in range(TOK):
                ins = pe.transpose(B[3][:, P * t:P * t + P], v_t[:, P * t:P * t + P], ident[:, :])
            ins.then_inc(v_turned, 1)
            pe.wait_ge(norm_sum, 2)
            pe.matmul(B[1][:, :], ones[:, :], t3[:, :], start=True, stop=True).then_inc(norm_total, 1)
            pe.wait_ge(norm_sum, 3)
            pe.matmul(B[2][:, :], ones[:, :], sq[:, 0, 0:SEQ], start=True, stop=True).then_inc(norm_total, 1)
            for s in range(8):
                c = QA0 + 8 + s
                pe.wait_ge(w_lo_ready, c + 1)
                for ct in range(4):
                    if s == 0:
                        if ct == 0:
                            pe.wait_ge(proj_evac, T_KR + 1)
                        if ct == 1:
                            pe.wait_ge(norm_root, 3)
                        if ct == 3:
                            pe.wait_ge(v_kept, 1)
                    columns(c, (0, 1, 2, 3), (ct,), (2 * s, 2 * s + 1), ct == 0)

            def a_score(t, u):
                i, m, slot = u // 2, u % 2, u % 2
                w = 2 * CHUNK if i == 0 else 3 * CHUNK
                pe.wait_ge(a_exp, A_UNITS * t + u + 1)
                k0 = P * (i + 1) - w
                for e in range(2):
                    dst = B[4 + slot][:, 192 * e + 192 - w:192 * e + 192]
                    q = qs[:, m, e, P * i:P * i + P]
                    pe.matmul(dst, q, ks_hi[:, k0:k0 + w], start=e == 0, stop=False)
                    pe.matmul(dst, q, ks_lo[:, k0:k0 + w], start=False, stop=False)
                both = B[4 + slot][:, 0:384].rearrange("p (a b) -> p a b", a=2)
                if i > 0:
                    pe.matmul(both[:, :, 0:CHUNK], ident_bf[:, :], mask_bf[:, 0, :, :], start=False, stop=False)
                pe.matmul(both[:, :, 2 * CHUNK:3 * CHUNK], ident_bf[:, :], mask_bf[:, 1, :, :], start=False, stop=True).then_inc(a_scores, 1)

            def a_transpose(t, u):
                i, slot = u // 2, u % 2
                pe.wait_ge(a_probs, A_UNITS * t + u + 1)
                pe.wait_ge(a_pt_lo, A_UNITS * t + u + 1)
                for e in range(2):
                    ins = pe.transpose(B[6][:, P * e:P * e + P], pa[:, slot, e, 2 * CHUNK:], ident[:, :])
                if i > 0:
                    for e in range(2):
                        ins = pe.transpose(B[6][:, 256 + P * e:256 + P * e + P], pa[:, slot, e, 0:2 * CHUNK], ident[:, :])
                ins.then_inc(a_turned, 1)

            def a_product(t, i):
                pe.wait_ge(a_pt_lo, A_UNITS * t + 2 * i + 3)
                pe.wait_ge(a_out, TOK * t + i + 1)
                dst = B[7][:, 0:256].rearrange("p (a b) -> p a b", a=2)
                for e in range(2):
                    ins = three(dst, va_hi[:, i, e, :], va_lo[:, i, e, :], pta_hi[:, :, P * e:P * e + P], pta_lo[:, :, P * e:P * e + P],
                                e == 0, i == 0 and e == 1)
                if i > 0:
                    for e in range(2):
                        o = 256 + CHUNK * e
                        ins = three(dst[:, :, 0:CHUNK], va_hi[:, i - 1, e, :], va_lo[:, i - 1, e, :],
                                    pta_hi[:, :, o:o + CHUNK], pta_lo[:, :, o:o + CHUNK], False, e == 1)
                ins.then_inc(a_pv, 1)

            pe.wait_ge(proj_evac, T_GT)
            pe.wait_ge(consts_set, 6)
            with pe.Fori(0, 4) as t:
                for hf in range(16):
                    if hf in AT_PV:
                        a_product(t, AT_PV[hf])
                    if hf in AT_TRANSPOSE:
                        a_transpose(t, AT_TRANSPOSE[hf])
                    if hf in AT_SCORES:
                        if AT_SCORES[hf] == 0:
                            pe.wait_ge(a_split_lo, t + 1)
                        a_score(t, AT_SCORES[hf])
                    s = hf // 2
                    if hf % 2 == 0:
                        pe.wait_ge(w_lo_ready, 8 * t + (GT0 + s + 1))
                    for ct in (0, 1) if hf % 2 == 0 else (2, 3):
                        if s == 0:
                            pe.wait_ge(proj_evac, 4 * t + (T_GT - 4 + ct + 1))
                        columns(GT0 + s, (0, 1, 2, 3), (ct,), (2 * s, 2 * s + 1), ct == 0)

            pe.wait_ge(proj_evac, T_GT + 16)
            pe.wait_ge(a_out, 17)
            with pe.Fori(0, 4) as p:
                ck, cqn, crt = PB0 % HL, (PB0 + 1) % HL, (PB0 + 2) % HL

                def b_tile(n, width_k, slot, off, step, rhs_hi, rhs_lo):
                    for k in range(width_k):
                        o = off + step * k
                        ins = three(B[n % 4][:, :], w_hi[:, slot, o:o + P], w_lo[:, slot, o:o + P], rhs_hi[:, k, :], rhs_lo[:, k, :],
                                    k == 0, k == width_k - 1, n == 0 and k == 0)
                    ins.then_inc(proj_done, 1)

                pe.wait_ge(w_lo_ready, 4 * p + (PB0 + 1))
                b_tile(0, CKV_T, ck, 0, 256, ckv_hi, ckv_lo)
                for half in range(2):
                    for tt in range(2):
                        tok = 2 * half + tt
                        for k in range(CKV_T):
                            o = 512 + 256 * k
                            ins = three(B[1 + half][:, 256 * tt:256 * tt + 256], ckv_hi[:, k, P * tok:P * tok + P], ckv_lo[:, k, P * tok:P * tok + P],
                                        w_hi[:, ck, o:o + 256], w_lo[:, ck, o:o + 256], k == 0, k == CKV_T - 1)
                    ins.then_inc(proj_done, 1)
                b_tile(3, CKV_T, ck, P, 256, ckv_hi, ckv_lo)
                pe.wait_ge(w_lo_ready, 4 * p + (PB0 + 3))
                pe.wait_ge(lat_lo, 2 + CQ_T)
                pe.wait_ge(proj_evac, PB_TILES * p + (T_PB + 1))
                b_tile(4, CQ_T, crt, 0, P, cqs_hi, cqs_lo)
                pe.wait_ge(proj_evac, PB_TILES * p + (T_PB + 2))
                b_tile(5, CQ_T, cqn, 0, 256, cqs_hi, cqs_lo)
                pe.wait_ge(proj_evac, PB_TILES * p + (T_PB + 3))
                b_tile(6, CQ_T, cqn, P, 256, cqs_hi, cqs_lo)

                def b_score(u):
                    h, i = u // 4, u % 4
                    n = P * (i + 1)
                    pe.wait_ge(b_exp, 8 * p + u + 1)
                    dst = B[4 + u % 2][:, 0:n]
                    q = slice(P * i, P * i + P)
                    ins = pe.matmul(dst, qr[:, h, q], kr_hi[:, 0:n], start=True, stop=False)
                    if u == 0:
                        ins.then_inc(w_used, 3)
                    pe.matmul(dst, qr[:, h, q], kr_lo[:, 0:n], start=False, stop=False)
                    three(dst, qn_hi[:, h, q], qn_lo[:, h, q], kn_hi[:, h, 0:n], kn_lo[:, h, 0:n], False, False)
                    pe.matmul(B[4 + u % 2][:, n - CHUNK:n], ident_bf[:, :], mask_bf[:, 1, 0, :], start=False, stop=True).then_inc(b_scores, 1)

                def b_transpose(u):
                    pe.wait_ge(b_probs, 8 * p + u + 1)
                    pe.wait_ge(b_pt_lo, 8 * p + u + 1)
                    for kt in range(u % 4 + 1):
                        ins = pe.transpose(B[(6, 3)[u % 2]][:, P * kt:P * kt + P], pb[:, u % 4, P * kt:P * kt + P], ident[:, :])
                    ins.then_inc(b_turned, 1)

                def b_product(h):
                    pe.wait_ge(b_pt_lo, 8 * p + 4 * h + 6)
                    pe.wait_ge(b_out, 2 * p + h + 1)
                    for kt in range(TOK):
                        ins = three(B[7][:, P * kt:SEQ], vb_hi[:, kt, P * h:P * h + P], vb_lo[:, kt, P * h:P * h + P],
                                    ptb_hi[:, kt, P * kt:SEQ], ptb_lo[:, kt, P * kt:SEQ], kt == 0, kt == TOK - 1)
                    ins.then_inc(b_pv, 1)

                pe.wait_ge(proj_evac, PB_TILES * p + (T_PB + PB_TILES))
                for u in range(4):
                    b_score(u)
                for u in range(4):
                    b_transpose(u)
                    b_score(4 + u)
                b_product(0)
                for u in range(4, 8):
                    b_transpose(u)
                b_product(1)

            def out_group(n):
                for s in range(8):
                    pe.wait_ge(w_lo_ready, 8 * n + (WO0 + s + 1))
                    pe.wait_ge(m_lo, s + 1)
                    for t in range(TOK):
                        if s == 0:
                            pe.wait_ge(o_evac, 4 * n + (t + 1))
                        for kk in range(2):
                            k = 2 * s + kk
                            mh, ml = (ma_hi, ma_lo) if k < A_TILES else (mb_hi, mb_lo)
                            kx = k % A_TILES
                            slot = (WO0 + s) % HL
                            ins = three(B[t][:, :], mh[:, kx, P * t:P * t + P], ml[:, kx, P * t:P * t + P],
                                        w_hi[:, slot, SEQ * kk:SEQ * kk + SEQ], w_lo[:, slot, SEQ * kk:SEQ * kk + SEQ],
                                        k == 0, k == MIX_TILES - 1, t == 0 and kk == 0)
                        if s == 7:
                            ins.then_inc(o_done, 1)

            with pe.Fori(0, 3) as n:
                out_group(n)
            out_group(3)


def laid_out_weights(w_in, w_q_b, w_kv_b, w_out):
    def cols(*parts):
        return np.concatenate(parts, axis=1)

    def chunked(w, ks):
        k, c = w.shape
        return w.reshape(k // (P * ks), ks, P, c).transpose(0, 2, 1, 3).reshape(-1, P, ks * c)

    a_w, kv_w = A_HEADS * A_DIM, A_KV_HEADS * A_DIM
    o = np.cumsum([0, a_w, kv_w, kv_w, a_w, Q_LORA, KV_LORA, B_ROPE, B_HEADS * B_V])
    a_q, a_k, a_v, a_g, b_cq, b_ckv, b_kr, b_g = (w_in[:, o[i]:o[i + 1]] for i in range(8))
    stream = [chunked(cols(a_k, a_v, b_ckv), 2), chunked(b_cq, 2), chunked(cols(b_kr, b_kr), 8),
              chunked(a_q[:, 0:SEQ], 2), chunked(a_q[:, SEQ:], 2)]
    for t in range(4):
        c = slice(2 * P * t, 2 * P * t + 2 * P)
        stream.append(chunked(cols(a_g[:, c], b_g[:, c]), 2))
    q = w_q_b.reshape(Q_LORA, B_HEADS, B_NOPE + B_ROPE)
    kv = w_kv_b.reshape(KV_LORA, B_HEADS, B_NOPE + B_V)
    pad = np.zeros((1, P, CE // 2), w_q_b.dtype)
    for p in range(B_HEADS // 2):
        h = slice(2 * p, 2 * p + 2)
        kn = chunked(kv[:, h, :B_NOPE].reshape(KV_LORA, -1), 2)
        v = chunked(kv[:, h, B_NOPE:].reshape(KV_LORA, -1), 2)
        qn = chunked(q[:, h, :B_NOPE].reshape(Q_LORA, -1), 4)
        qr = chunked(q[:, h, B_NOPE:].reshape(Q_LORA, -1), 4)
        stream += [np.concatenate([kn, v], axis=2), qn, np.concatenate([qr, pad], axis=2), np.concatenate([pad, pad], axis=2)]
    for n in range(4):
        stream.append(chunked(w_out[:, SEQ * n:SEQ * n + SEQ], 2))
    stream = np.concatenate(stream, axis=0)
    assert stream.shape == (CHUNKS, P, CE)
    return np.ascontiguousarray(stream)


def rotary_tables():
    half = A_DIM // 2
    inv_freq = np.float32(1) / (np.float32(10000.0) ** (np.arange(0, A_DIM, 2, dtype=np.float32) / np.float32(A_DIM)))
    ang = np.arange(SEQ, dtype=np.float32)[None, :] * inv_freq.astype(np.float32)[:, None]
    cos, sin = np.cos(ang.astype(np.float64)), np.sin(ang.astype(np.float64))
    assert half == 32 and A_DIM == B_ROPE
    cos = np.concatenate([cos] * 4, axis=0)
    sin = np.concatenate([-sin, sin] * 2, axis=0)
    return np.ascontiguousarray(np.concatenate([np.eye(P), cos, sin], axis=1).astype(np.float32))


def kernel(x, norm_in_w, w_in, sinks_a, q_a_norm_w, w_q_b, kv_a_norm_w, w_kv_b, w_out, final_norm_w):
    import concourse.bacc as bacc
    from concourse.bass_utils import run_bass_kernel_spmd

    x, norm_in_w, w_in, sinks_a, q_a_norm_w, w_q_b, kv_a_norm_w, w_kv_b, w_out, final_norm_w = (
        np.asarray(a) for a in (x, norm_in_w, w_in, sinks_a, q_a_norm_w, w_q_b, kv_a_norm_w, w_kv_b, w_out, final_norm_w))
    arrays = {
        "w_stream": laid_out_weights(w_in, w_q_b, w_kv_b, w_out),
        "x_t": np.ascontiguousarray(x[0].T.reshape(8, 2, P, SEQ).transpose(0, 2, 1, 3).reshape(8, P, CE)),
        "x_nat": np.ascontiguousarray(x),
        "gains": np.ascontiguousarray(np.concatenate(
            [norm_in_w.reshape(K_IN, P).T, q_a_norm_w.reshape(CQ_T, P).T, kv_a_norm_w.reshape(CKV_T, P).T,
             np.broadcast_to(sinks_a[None, :], (P, A_HEADS))], axis=1)),
        "final_w": np.ascontiguousarray(np.broadcast_to(final_norm_w[None, :], (P, D_MODEL))),
        "tables": rotary_tables(),
    }
    nc = bacc.Bacc("TRN2", target_bir_lowering=False, num_devices=1)
    args = [nc.dram_tensor(name, a.shape, mybir.dt.from_np(a.dtype), kind="ExternalInput").ap() for name, a in arrays.items()]
    args.append(nc.dram_tensor("out", (1, SEQ, D_MODEL), F32, kind="ExternalOutput").ap())
    build(nc, *args)
    r = run_bass_kernel_spmd(nc, [arrays], core_ids=[0])
    return r.results[0]["out"]
```

```python
from contextlib import ExitStack

import concourse.bass as bass
import numpy as np
from concourse import mybir

ALU = mybir.AluOpType
ACT = mybir.ActivationFunctionType
AX = mybir.AxisListType
F32 = mybir.dt.float32
F32R = mybir.dt.float32r
BF16 = mybir.dt.bfloat16

P = 128
D_MODEL, SEQ = 2048, 512
CHUNK = 64
EPS = 1e-6
MASK_VALUE = -1e30
A_HEADS, A_KV_HEADS, A_DIM = 16, 2, 64
B_HEADS, B_NOPE, B_ROPE, B_V = 8, 128, 64, 128
Q_LORA, KV_LORA = 512, 256
A_SCALE = A_DIM ** -0.5
B_SCALE = (B_NOPE + B_ROPE) ** -0.5
K_IN = D_MODEL // P
TOK = SEQ // P
A_TILES = A_HEADS * A_DIM // P
B_TILES = B_HEADS * B_V // P
MIX_TILES = A_TILES + B_TILES
CQ_T, CKV_T = Q_LORA // P, KV_LORA // P

CE = 1024
KV0 = 0
CQ0 = KV0 + 8
QA0 = CQ0 + 8
KR0 = QA0 + 16
GT0 = KR0 + 2
PB0 = GT0 + 32
WO0 = PB0 + 12
CHUNKS = WO0 + 32
RAW, HL = 2, 4
AHEAD = 3

T_CQ, T_QA, T_KR, T_GT = 4, 8, 16, 17
T_PB = T_GT + 16
PAIRS = B_HEADS // 2
PB_TILES = 7

A_UNITS = 8
AT_SCORES = {4: 0, 5: 1, 7: 2, 8: 3, 9: 4, 11: 5, 12: 6, 13: 7}
AT_TRANSPOSE = {6: 0, 7: 1, 9: 2, 10: 3, 11: 4, 13: 5, 14: 6, 15: 7}
AT_PV = {8: 0, 11: 1, 14: 2, 16: 3}

B_STEPS = ("S0 F S1 F S2 F T0 S3 F T1 S4 F T2 S5 F T3 S6 F V0 S7 F T4 T5 F T6 F T7 F V1").split()
B_PIECES = [((0, (0, 1)),), ((1, (0, 1)),), ((2, (0, 1)),), ((3, (0, 1)),), ((4, (0, 1)),), ((4, (2, 3)),), ((5, (0, 1)),),
            ((5, (2, 3)),), ((6, (0, 1)),), ((6, (2, 3)),), ()]
CHUNK_OF_TILE = (0, 0, 0, 0, 1, 2, 2)
OUT_PIECES = [2, 2, 1, 1, 1, 1, 2, 2, 2, 1, 1]


def build(nc, w_stream, x_t, x_nat, gains, final_w, tables, out):
    with ExitStack() as ctx:
        def sem(name):
            return ctx.enter_context(nc.semaphore(name))

        def bank(name):
            return ctx.enter_context(nc.psum_tensor(name, [P, 512], F32))

        base = (nc.sbuf_base + 31) // 32 * 32
        place = [base]

        def at(name, shape, dt, offset):
            return nc.alloc_sbuf_tensor_at(name, shape, dt, offset=offset)

        def region(nbytes):
            start = place[0]
            place[0] += (nbytes + 31) // 32 * 32
            return start

        r_x = region(2 * K_IN * SEQ * 4)
        x_hi = at("x_hi", [P, K_IN, SEQ], F32R, r_x)
        x_lo = at("x_lo", [P, K_IN, SEQ], F32R, r_x + K_IN * SEQ * 4)
        KB = 1024
        cqs_hi = at("cqs_hi", [P, CQ_T, SEQ], F32R, r_x + 32 * KB)
        cqs_lo = at("cqs_lo", [P, CQ_T, SEQ], F32R, r_x + 40 * KB)
        ptb_hi = at("ptb_hi", [P, TOK, SEQ], F32R, r_x + 48 * KB)
        ptb_lo = at("ptb_lo", [P, TOK, SEQ], F32R, r_x + 56 * KB)

        r_mixed = region(MIX_TILES * SEQ * 4)
        mixed = at("mixed", [P, MIX_TILES, SEQ], F32, r_mixed)

        w_raw = at("w_raw", [P, RAW, CE], F32, region(RAW * CE * 4))
        w_hi = at("w_hi", [P, HL, CE], F32R, region(HL * CE * 4))
        w_lo = at("w_lo", [P, HL, CE], F32R, region(HL * CE * 4))

        gain = at("gain", [P, 38], F32, region(38 * 4))
        g_in, g_q, g_kv, sinks = gain[:, 0:16], gain[:, 16:20], gain[:, 20:22], gain[:, 22:38]
        neg_sinks = at("neg_sinks", [P, A_HEADS], F32, region(64))
        eps = at("eps", [P, 1], F32, region(4))
        ident = at("ident", [P, P], F32, region(512))
        ones = at("ones", [P, P], F32, region(512))
        ident_bf = at("ident_bf", [P, P], BF16, region(256))
        mask_bf = at("mask_bf", [P, 2, 2, CHUNK], BF16, region(512))
        st_a = at("st_a", [P, 2, 6, 2], F32, region(96))
        st_b = at("st_b", [P, 4, 4], F32, region(64))
        sumsq = at("sumsq", [P, TOK, 4], F32, region(64))
        fin = at("fin", [P, TOK, 3], F32, region(48))
        rstd = at("rstd", [P, SEQ], F32, region(2048))
        r_rot = region(4096)
        cos_r = at("cos_r", [P, SEQ], F32, r_rot)
        sin_r = at("sin_r", [P, SEQ], F32, r_rot + 2048)
        gate_tmp = at("gate_tmp", [P, 2, SEQ], F32, r_rot)
        cos_b = at("cos_b", [P, SEQ], F32, r_rot)
        sin_b = at("sin_b", [P, SEQ], F32, r_rot + 2048)
        r_ckv = region(8192)
        ckv_hi = at("ckv_hi", [P, CKV_T, SEQ], F32R, r_ckv)
        ckv_lo = at("ckv_lo", [P, CKV_T, SEQ], F32R, r_ckv + 4096)
        fw = at("fw", [P, D_MODEL], F32, r_ckv)
        r_cq = region(8192)
        cq = at("cq", [P, CQ_T, SEQ], F32, r_cq)
        kr_hi = at("kr_hi", [P, SEQ], F32R, region(2048))
        kr_lo = at("kr_lo", [P, SEQ], F32R, region(2048))
        r_tmp = region(6144)
        t1 = at("t1", [P, SEQ], F32, r_tmp)
        t2 = at("t2", [P, SEQ], F32, r_tmp + 2048)
        t3 = at("t3", [P, SEQ], F32, r_tmp + 4096)
        r4 = region(36 * KB)
        xs = at("xs", [P, 2, CE], F32, r4)
        sq = at("sq", [P, 2, CE], F32, r4 + 8 * KB)
        acc = at("acc", [P, CE], F32, r4 + 16 * KB)
        ckv = at("ckv", [P, CKV_T, SEQ], F32, r4 + 20 * KB)
        v_t = at("v_t", [P, SEQ], F32, r4 + 24 * KB)
        qs = at("qs", [P, 2, 2, SEQ], F32R, r4)
        ks_hi = at("ks_hi", [P, SEQ], F32R, r4 + 8 * KB)
        ks_lo = at("ks_lo", [P, SEQ], F32R, r4 + 10 * KB)
        va_hi = at("va_hi", [P, TOK, 2, P], F32R, r4 + 12 * KB)
        va_lo = at("va_lo", [P, TOK, 2, P], F32R, r4 + 16 * KB)
        pa = at("pa", [P, 2, 2, 4 * CHUNK], F32, r4 + 20 * KB)
        pta_hi = at("pta_hi", [P, 2, 384], F32R, r4 + 24 * KB)
        pta_lo = at("pta_lo", [P, 2, 384], F32R, r4 + 27 * KB)
        k_dup = at("k_dup", [P, A_KV_HEADS, SEQ], F32, r4 + 30 * KB)
        v_f = at("v_f", [P, TOK, P], F32, r4 + 34 * KB)
        qn_hi, qn_lo, kn_hi, kn_lo, qr, vb_hi, vb_lo = ([] for _ in range(7))
        for par, r in enumerate((r_x, r4)):
            for n, (kept, name) in enumerate(((qn_hi, "qn_hi"), (qn_lo, "qn_lo"), (kn_hi, "kn_hi"), (kn_lo, "kn_lo"), (qr, "qr"))):
                kept.append(at(f"{name}{par}", [P, 2, SEQ], F32R, r + 4 * KB * n))
            vb_hi.append(at(f"vb_hi{par}", [P, TOK, 2 * P], F32R, r + 20 * KB))
            vb_lo.append(at(f"vb_lo{par}", [P, TOK, 2 * P], F32R, r + 24 * KB))
        pb = at("pb", [P, 4, SEQ], F32, r4 + 28 * KB)
        m_at = [r_x, r_x + 8 * KB, r_x + 16 * KB, r_x + 24 * KB, r_x + 32 * KB, r_x + 40 * KB, r_cq, r_x + 48 * KB]
        mx_hi = [at(f"mx_hi{j}", [P, 2, SEQ], F32R, o) for j, o in enumerate(m_at)]
        mx_lo = [at(f"mx_lo{j}", [P, 2, SEQ], F32R, o + 4 * KB) for j, o in enumerate(m_at)]
        y = at("y", [P, TOK, D_MODEL], F32, r4)
        junk = at("junk", [P, SEQ], F32, r4 + 32 * KB)
        assert place[0] <= nc.sbuf_usable_end, place[0]

        B = [bank(f"bank{i}") for i in range(8)]

        w_landed = [sem(f"w_landed{i}") for i in range(RAW)]
        w_hi_ready, w_lo_ready, w_used = sem("w_hi_ready"), sem("w_lo_ready"), sem("w_used")
        x_landed = [sem("x_landed0"), sem("x_landed1")]
        x_hi_ready, x_lo_ready, x_squared, x_summed = sem("x_hi_ready"), sem("x_lo_ready"), sem("x_squared"), sem("x_summed")
        gains_landed, tables_landed, rot_landed = sem("gains_landed"), sem("tables_landed"), sem("rot_landed")
        y0_landed, y_landed = sem("y0_landed"), sem("y_landed")
        consts_set = sem("consts_set")
        norm_sum, norm_total, norm_root, norm_recip = sem("norm_sum"), sem("norm_total"), sem("norm_root"), sem("norm_recip")
        proj_done, proj_evac = sem("proj_done"), sem("proj_evac")
        rot_terms, rotated, lat_scaled, lat_hi, lat_lo = sem("rot_terms"), sem("rotated"), sem("lat_scaled"), sem("lat_hi"), sem("lat_lo")
        v_turned, v_kept, squares = sem("v_turned"), sem("v_kept"), sem("squares")
        a_zeroed, a_split_hi, a_split_lo = sem("a_zeroed"), sem("a_split_hi"), sem("a_split_lo")
        a_scores, a_max, a_shift, a_exp, a_recip, a_probs = sem("a_scores"), sem("a_max"), sem("a_shift"), sem("a_exp"), sem("a_recip"), sem("a_probs")
        a_turned, a_pt_hi, a_pt_lo, a_pv, a_out = sem("a_turned"), sem("a_pt_hi"), sem("a_pt_lo"), sem("a_pv"), sem("a_out")
        gate_silu, gated = sem("gate_silu"), sem("gated")
        b_hi, b_rot, b_lo = sem("b_hi"), sem("b_rot"), sem("b_lo")
        b_scores, b_max, b_shift, b_exp, b_recip, b_probs = sem("b_scores"), sem("b_max"), sem("b_shift"), sem("b_exp"), sem("b_recip"), sem("b_probs")
        b_turned, b_pt_hi, b_pt_lo, b_pv, b_out = sem("b_turned"), sem("b_pt_hi"), sem("b_pt_lo"), sem("b_pv"), sem("b_out")
        m_hi, m_lo = sem("m_hi"), sem("m_lo")
        o_done, o_evac, o_squared, o_gained, o_sum, o_root = sem("o_done"), sem("o_evac"), sem("o_squared"), sem("o_gained"), sem("o_sum"), sem("o_root")
        o_recip, o_scaled, o_scaled_act, stored = sem("o_recip"), sem("o_scaled"), sem("o_scaled_act"), sem("stored")

        block = ctx.enter_context(nc.Block())

        @block.sync
        def _(sp):
            for j in range(8):
                if j >= 2:
                    sp.wait_ge(x_lo_ready, j - 1)
                    sp.wait_ge(x_squared, j - 1)
                sp.dma_start(xs[:, j % 2, :], x_t[j, :, :]).then_inc(x_landed[j % 2], 16)
                if j >= RAW:
                    sp.wait_ge(w_lo_ready, j - 1)
                sp.dma_start(w_raw[:, j % RAW, :], w_stream[j, :, :]).then_inc(w_landed[j % RAW], 16)
            with sp.Fori(0, (CHUNKS - 8) // RAW) as i:
                for s in range(RAW):
                    sp.wait_ge(w_lo_ready, RAW * i + (7 + s))
                    sp.dma_start(w_raw[:, s, :], w_stream[bass.ds(RAW * i + (8 + s), 1), :, :].rearrange("a p c -> (a p) c"))\
                        .then_inc(w_landed[s], 16)
            for t in range(TOK):
                sp.wait_ge(o_scaled_act, t + 1)
                sp.dma_start(out[0, P * t:P * t + P, 0:CE], y[:, t, 0:CE]).then_inc(stored, 16)
                sp.wait_ge(o_scaled, t + 1)
                sp.dma_start(out[0, P * t:P * t + P, CE:], y[:, t, CE:]).then_inc(stored, 16)
            sp.wait_ge(stored, 16 * 2 * TOK)

        @block.gpsimd
        def _(pool):
            def low_part(c, s):
                pool.wait_ge(w_hi_ready, c + 1)
                pool.tensor_tensor(w_lo[:, s % HL, :], w_raw[:, s % RAW, :], w_hi[:, s % HL, :].bitcast(F32), ALU.subtract)\
                    .then_inc(w_lo_ready, 1)

            head = WO0 + 8
            with pool.Fori(0, head // HL) as i:
                for s in range(HL):
                    low_part(HL * i + s, s)
            for c in range(head // HL * HL, head):
                low_part(c, c)
            with pool.Fori(0, 3) as n:
                for s in range(8):
                    low_part(8 * n + (head + s), head + s)
                    if s == 4:
                        pool.wait_ge(y_landed, 16 * 4)
                        for t in range(TOK):
                            pool.wait_ge(o_squared, 4 * n + (t + 2))
                            cols = bass.ds(SEQ * n, SEQ)
                            pool.tensor_tensor(y[:, t, cols], y[:, t, cols], fw[:, cols], ALU.mult).then_inc(o_gained, 1)

        @block.scalar
        def _(act):
            def high_part(c, s):
                act.wait_ge(w_landed[s % RAW], 8 * (c - s % RAW) + 16)
                if not isinstance(c, int) or c >= HL:
                    act.wait_ge(w_used, c - (HL - 1))
                act.activation(w_hi[:, s % HL, :], w_raw[:, s % RAW, :], ACT.Copy).then_inc(w_hi_ready, 1)

            def x_parts(j):
                act.wait_ge(x_landed[j % 2], 16 * (j // 2 + 1))
                for h in range(2):
                    k = 2 * j + h
                    ins = act.activation(x_hi[:, k, :], xs[:, j % 2, SEQ * h:SEQ * h + SEQ], ACT.Copy, scale=g_in[:, k:k + 1])
                ins.then_inc(x_hi_ready, 1)
                if j >= 3:
                    act.wait_ge(x_summed, j - 2)
                act.activation(acc[:, :] if j == 0 else sq[:, j % 2, :], xs[:, j % 2, :], ACT.Square).then_inc(x_squared, 1)

            act.dma_start(gain[:, :], gains[:, :]).then_inc(gains_landed, 16)
            act.dma_start(ident[:, :], tables[:, 0:P]).then_inc(tables_landed, 16)
            act.dma_start(cos_r[:, :], tables[:, P:P + SEQ]).then_inc(tables_landed, 16)
            act.dma_start(sin_r[:, :], tables[:, P + SEQ:P + 2 * SEQ]).then_inc(tables_landed, 16)
            act.sem_inc(a_exp, 2)
            act.sem_inc(b_exp, 2)
            act.wait_ge(gains_landed, 16)
            high_part(0, 0)
            x_parts(0)
            high_part(1, 1)
            x_parts(1)
            high_part(2, 2)

            def root(n, total, width):
                act.wait_ge(norm_total, n)
                act.wait_ge(consts_set, 1)
                act.activation(t2[:, :], total, ACT.Sqrt, bias=eps[:, :], scale=1.0 / width).then_inc(norm_root, 1)

            for c in range(GT0):
                if c + 2 < 8:
                    x_parts(c + 2)
                high_part(c + AHEAD, c + AHEAD)
                if c == CQ0:
                    root(1, B[7][:, :], D_MODEL)
                if c == QA0:
                    act.wait_ge(proj_evac, T_QA)
                    act.activation(sq[:, 0, :], ckv[:, :, :].rearrange("p a b -> p (a b)"), ACT.Square).then_inc(squares, 1)
                    act.activation(sq[:, 1, :], cq[:, 0:2, :].rearrange("p a b -> p (a b)"), ACT.Square).then_inc(squares, 1)
                    act.wait_ge(norm_sum, 1)
                    act.activation(acc[:, :], cq[:, 2:4, :].rearrange("p a b -> p (a b)"), ACT.Square).then_inc(squares, 1)
                if c == QA0 + 4:
                    root(2, B[4][:, :], KV_LORA)
                    act.wait_ge(norm_recip, 2)
                    root(3, B[5][:, :], Q_LORA)
                    act.wait_ge(lat_scaled, 1)
                    act.activation(ckv_hi[:, :, :], ckv[:, :, :], ACT.Copy).then_inc(lat_hi, 1)

            def a_split(t):
                act.wait_ge(a_pv, 4 * t + 1)
                act.activation(qs[0:64, :, 0, :], mixed[0:64, bass.ds(2 * t, 2), :], ACT.Copy)
                act.activation(qs[64:128, :, 1, :], mixed[64:128, bass.ds(2 * t, 2), :], ACT.Copy).then_inc(a_split_hi, 1)
                g = t // 2
                act.activation(ks_hi[:, :], k_dup[:, bass.ds(g, 1), :].rearrange("p a b -> p (a b)"), ACT.Copy)
                act.activation(va_hi[:, :, 0, 0:64], v_f[:, :, bass.ds(64 * g, 64)], ACT.Copy)
                act.activation(va_hi[:, :, 1, 64:128], v_f[:, :, bass.ds(64 * g, 64)], ACT.Copy).then_inc(a_split_hi, 1)

            def a_exps(t, u):
                i, slot = u // 2, u % 2
                w = 2 * CHUNK if i == 0 else 3 * CHUNK
                act.wait_ge(a_turned, A_UNITS * t + u + 1)
                act.wait_ge(a_shift, A_UNITS * t + u + 1)
                st = st_a[:, slot, :, :]
                for e in range(2):
                    act.activation(pa[:, slot, e, 4 * CHUNK - w:], B[4 + slot][:, 192 * e + 192 - w:192 * e + 192], ACT.Exp,
                                   bias=st[:, 1, e:e + 1], scale=A_SCALE, accum_out=st[:, 3, e:e + 1])
                act.activation(st[:, 4, :], st[:, 2, :], ACT.Exp).then_inc(a_exp, 1)

            def a_pt_high(t, u):
                i, m = u // 2, u % 2
                act.wait_ge(a_turned, A_UNITS * t + u + 3)
                if m == 0:
                    act.wait_ge(a_pv, TOK * t + i + 1)
                ins = act.activation(pta_hi[:, m, 0:256], B[6][:, 0:256], ACT.Copy)
                if i > 0:
                    ins = act.activation(pta_hi[:, m, 256:384].rearrange("p (a b) -> p a b", a=2),
                                   B[6][:, 256:512].rearrange("p (a b) -> p a b", a=2)[:, :, 0:64], ACT.Copy)
                ins.then_inc(a_pt_hi, 1)

            act.wait_ge(a_zeroed, 1)
            act.wait_ge(v_kept, 1)
            act.wait_ge(rotated, 10)
            act.activation(kr_hi[:, :], t3[:, :], ACT.Copy).then_inc(lat_hi, 1)
            with act.Fori(0, 4) as t:
                for hf in range(16):
                    if hf == 0:
                        a_split(t)
                    if hf % 2 == 0:
                        high_part(8 * t + (GT0 + AHEAD + hf // 2), GT0 + AHEAD + hf // 2)
                    if hf in AT_TRANSPOSE:
                        a_pt_high(t, AT_TRANSPOSE[hf])
                    if hf in AT_SCORES:
                        a_exps(t, AT_SCORES[hf])
                for ct in range(4):
                    act.wait_ge(proj_evac, 4 * t + (T_GT + ct + 1))
                    dst = gate_tmp[:, ct, :] if ct < 2 else mixed[:, bass.ds(2 * t + (A_TILES + ct - 2), 1), :].rearrange("p a b -> p (a b)")
                    act.activation(dst, dst, ACT.Silu).then_inc(gate_silu, 1)

            act.wait_ge(gated, 8)
            act.dma_start(cos_b[:, :], tables[:, P:P + SEQ]).then_inc(rot_landed, 16)
            act.dma_start(sin_b[:, :], tables[:, P + SEQ:P + 2 * SEQ]).then_inc(rot_landed, 16)
            act.wait_ge(w_used, PB0)
            for k in range(CQ_T):
                act.activation(cqs_hi[:, k, :], cq[:, k, :], ACT.Copy).then_inc(lat_hi, 1)

            def b_tile_high(idx):
                p, j = divmod(idx, PB_TILES)
                par, bk = p % 2, B[idx % 4]
                if j == 4:
                    act.wait_ge(b_rot, p + 1)
                    act.activation(qr[par][0:64, 0, :], t3[0:64, :], ACT.Copy)
                    act.activation(qr[par][64:128, 1, :], t3[64:128, :], ACT.Copy).then_inc(b_hi, 1)
                    return
                act.wait_ge(proj_done, T_PB + idx + 1)
                if j in (1, 2):
                    dst, src = vb_hi[par][:, 2 * j - 2:2 * j, :], bk[:, :].rearrange("p (a b) -> p a b", a=2)
                else:
                    dst, src = {0: kn_hi, 3: kn_hi, 5: qn_hi, 6: qn_hi}[j][par][:, {0: 0, 3: 1, 5: 0, 6: 1}[j], :], bk[:, :]
                act.activation(dst, src, ACT.Copy).then_inc(b_hi, 1)

            def b_expo(w):
                u = w % 8
                n = P * (u % 4 + 1)
                act.wait_ge(b_turned, w + 1)
                act.wait_ge(b_shift, w + 1)
                act.activation(pb[:, u % 4, 0:n], B[4 + u % 2][:, 0:n], ACT.Exp, bias=st_b[:, u % 4, 1:2], scale=B_SCALE,
                               accum_out=st_b[:, u % 4, 2:3]).then_inc(b_exp, 1)

            def b_pt_high(w):
                i = w % 4
                act.wait_ge(b_turned, w + 5)
                if i == 0:
                    act.wait_ge(b_pv, w // 4 + 1)
                act.activation(ptb_hi[:, 0:i + 1, P * i:P * i + P], B[6][:, 0:P * (i + 1)].rearrange("p (a b) -> p a b", a=i + 1),
                               ACT.Copy).then_inc(b_pt_hi, 1)

            def mixed_high(j):
                if j < 4:
                    act.wait_ge(b_pv, 7)
                elif j < 6:
                    act.wait_ge(proj_done, T_PB + PAIRS * PB_TILES)
                elif j == 7:
                    act.wait_ge(b_pv, 9)
                if j >= 4:
                    act.wait_ge(b_out, 2 * (j - 4) + 3)
                act.activation(mx_hi[j][:, :, :], mixed[:, 2 * j:2 * j + 2, :], ACT.Copy).then_inc(m_hi, 1)

            for j in range(PB_TILES):
                if j in (0, 4, 5):
                    c = PB0 + CHUNK_OF_TILE[j] + AHEAD
                    high_part(c, c)
                b_tile_high(j)
            for p in range(PAIRS):
                f = 0
                for step in B_STEPS:
                    w = 8 * p + (int(step[1]) if step[0] in "ST" else 0)
                    if step[0] == "S":
                        b_expo(w)
                    elif step[0] == "T":
                        b_pt_high(w)
                    elif step[0] == "F":
                        if p < PAIRS - 1:
                            for j, ks in B_PIECES[f]:
                                if ks[0] == 0 and j in (0, 4, 5):
                                    c = PB0 + 3 * (p + 1) + CHUNK_OF_TILE[j] + AHEAD
                                    high_part(c, c)
                                if ks[-1] == (1 if j < 4 else 3):
                                    b_tile_high(PB_TILES * (p + 1) + j)
                        else:
                            if f < 7:
                                mixed_high(f)
                            done = sum(OUT_PIECES[:f])
                            for piece in range(done, done + OUT_PIECES[f]):
                                if piece % 4 == 0:
                                    c = WO0 + piece // 4 + AHEAD
                                    high_part(c, c)
                        f += 1

            act.wait_ge(b_pv, 9)
            for n in range(4):
                act.dma_start(y[:, :, SEQ * n:SEQ * n + SEQ], x_nat[0, :, SEQ * n:SEQ * n + SEQ].rearrange("(t p) d -> p t d", p=P))\
                    .then_inc(y0_landed if n == 0 else y_landed, 16)
            act.dma_start(fw[:, :], final_w[:, :]).then_inc(y_landed, 16)
            mixed_high(7)

            def out_squares(n):
                for t in range(TOK):
                    act.wait_ge(o_evac, 4 * n + (t + 5))
                    act.wait_ge(o_squared, 4 * n + (t + 1))
                    act.activation(junk[:, :], y[:, t, bass.ds(SEQ * n, SEQ)], ACT.Square, accum_out=sumsq[:, t, bass.ds(n, 1)]).then_inc(o_squared, 1)

            act.sem_inc(o_squared, 1)
            for s in range(4, 8):
                c = WO0 + AHEAD + s
                high_part(c, c)
            out_squares(0)
            with act.Fori(1, 3) as n:
                for s in range(8):
                    high_part(8 * n + (WO0 + AHEAD + s), WO0 + AHEAD + s)
                out_squares(n)
            for s in range(8 - AHEAD):
                c = WO0 + 24 + AHEAD + s
                high_part(c, c)
            for t in range(TOK):
                act.wait_ge(o_evac, 12 + t + 5)
                act.wait_ge(o_squared, 12 + t + 1)
                act.activation(junk[:, :], y[:, t, 3 * SEQ:], ACT.Square, accum_out=sumsq[:, t, 3:4]).then_inc(o_squared, 1)
                act.wait_ge(o_sum, t + 1)
                act.activation(fin[:, t, 1:2], fin[:, t, 0:1], ACT.Sqrt, bias=eps[:, :], scale=1.0 / D_MODEL).then_inc(o_root, 1)
                act.wait_ge(o_recip, t + 1)
                act.wait_ge(o_gained, 8 + t + 1 if t < 3 else 12)
                act.activation(y[:, t, 0:CE], y[:, t, 0:CE], ACT.Copy, scale=fin[:, t, 2:3]).then_inc(o_scaled_act, 1)

        @block.vector
        def _(dve):
            dve.memset(eps[:, :], EPS).then_inc(consts_set, 1)
            dve.memset(ones[:, :], 1.0).then_inc(consts_set, 1)
            dve.memset(mask_bf[:, :, :, :], 0.0).then_inc(consts_set, 1)
            dve.wait_ge(consts_set, 3)
            dve.memset(mask_bf[64:128, 0, :, :], MASK_VALUE)
            dve.memset(mask_bf[0:64, 1, :, :], MASK_VALUE).then_inc(consts_set, 1)
            dve.sem_inc(a_pt_lo, 1)
            dve.sem_inc(a_out, 1)
            dve.sem_inc(b_pt_lo, 1)
            dve.sem_inc(b_out, 1)
            dve.sem_inc(o_evac, 4)
            dve.wait_ge(gains_landed, 16)
            dve.tensor_scalar(neg_sinks[:, :], sinks, -1.0, None, ALU.mult).then_inc(consts_set, 1)
            dve.wait_ge(tables_landed, 48)
            dve.tensor_copy(ident_bf[:, :], ident[:, :]).then_inc(consts_set, 1)

            for j in range(8):
                dve.wait_ge(x_hi_ready, j + 1)
                for h in range(2):
                    k = 2 * j + h
                    ins = dve.scalar_tensor_tensor(out=x_lo[:, k, :], in0=xs[:, j % 2, SEQ * h:SEQ * h + SEQ], scalar=g_in[:, k:k + 1],
                                                   op0=ALU.mult, in1=x_hi[:, k, :].bitcast(F32), op1=ALU.subtract)
                ins.then_inc(x_lo_ready, 1)
                if j >= 1:
                    dve.wait_ge(x_squared, j + 1)
                    if j >= 2:
                        dve.wait_ge(x_summed, j - 1)
                    dve.tensor_tensor(acc[:, :], acc[:, :], sq[:, j % 2, :], ALU.add).then_inc(x_summed, 1)
            dve.wait_ge(x_summed, 7)
            dve.tensor_tensor(t1[:, :], acc[:, 0:SEQ], acc[:, SEQ:CE], ALU.add).then_inc(norm_sum, 1)
            dve.wait_ge(norm_root, 1)
            dve.reciprocal(rstd[:, :], t2[:, :]).then_inc(norm_recip, 1)
            dve.wait_ge(norm_recip, 1)
            dve.tensor_tensor(cos_r[:, :], cos_r[:, :], rstd[:, :], ALU.mult)
            dve.tensor_tensor(sin_r[:, :], sin_r[:, :], rstd[:, :], ALU.mult).then_inc(consts_set, 1)
            dve.wait_ge(consts_set, 7)

            def rotate_terms(src, cos, sin, count):
                dve.tensor_tensor(t1[:, :], src[:, :], cos[:, :], ALU.mult)
                for q in range(4):
                    o = q ^ 1
                    ins = dve.tensor_tensor(t2[32 * q:32 * q + 32, :], src[32 * o:32 * o + 32, :], sin[32 * q:32 * q + 32, :], ALU.mult)
                ins.then_inc(proj_evac, 1)
                dve.wait_ge(proj_evac, count)

            dve.wait_ge(proj_done, 1)
            rotate_terms(B[0], cos_r, sin_r, 1)
            for g in range(A_KV_HEADS):
                for h in range(2):
                    ins = dve.tensor_tensor(k_dup[64 * h:64 * h + 64, g, :], t1[64 * g:64 * g + 64, :], t2[64 * g:64 * g + 64, :], ALU.add)
            ins.then_inc(rotated, 1)
            dve.wait_ge(proj_done, 2)
            dve.tensor_tensor(v_t[:, :], B[1][:, :], rstd[:, :], ALU.mult).then_inc(proj_evac, 1)
            for j in range(CKV_T):
                dve.wait_ge(proj_done, 3 + j)
                dve.tensor_tensor(ckv[:, j, :], B[2 + j][:, :], rstd[:, :], ALU.mult).then_inc(proj_evac, 1)
            for j in range(CQ_T):
                dve.wait_ge(proj_done, T_CQ + 1 + j)
                dve.tensor_tensor(cq[:, j, :], B[4 + j][:, :], rstd[:, :], ALU.mult).then_inc(proj_evac, 1)
            dve.wait_ge(squares, 3)
            dve.tensor_tensor(t3[:, :], sq[:, 0, 0:SEQ], sq[:, 0, SEQ:CE], ALU.add).then_inc(norm_sum, 1)
            dve.tensor_tensor(sq[:, 1, :], sq[:, 1, :], acc[:, :], ALU.add).then_inc(squares, 1)
            dve.wait_ge(squares, 4)
            dve.wait_ge(norm_sum, 2)
            dve.tensor_tensor(sq[:, 0, 0:SEQ], sq[:, 1, 0:SEQ], sq[:, 1, SEQ:CE], ALU.add).then_inc(norm_sum, 1)
            dve.wait_ge(norm_root, 2)
            dve.reciprocal(t3[:, :], t2[:, :]).then_inc(norm_recip, 1)
            dve.wait_ge(norm_recip, 2)
            for j in range(CKV_T):
                ins = dve.scalar_tensor_tensor(out=ckv[:, j, :], in0=ckv[:, j, :], scalar=g_kv[:, j:j + 1], op0=ALU.mult,
                                               in1=t3[:, :], op1=ALU.mult)
            ins.then_inc(lat_scaled, 1)
            dve.wait_ge(norm_root, 3)
            dve.wait_ge(lat_scaled, 1)
            dve.reciprocal(t3[:, :], t2[:, :]).then_inc(norm_recip, 1)
            dve.wait_ge(norm_recip, 3)
            for j in range(CQ_T):
                ins = dve.scalar_tensor_tensor(out=cq[:, j, :], in0=cq[:, j, :], scalar=g_q[:, j:j + 1], op0=ALU.mult,
                                               in1=t3[:, :], op1=ALU.mult)
            ins.then_inc(lat_scaled, 1)
            dve.wait_ge(lat_hi, 1)
            dve.tensor_tensor(ckv_lo[:, :, :], ckv[:, :, :], ckv_hi[:, :, :].bitcast(F32), ALU.subtract).then_inc(lat_lo, 1)
            dve.wait_ge(v_turned, 1)
            dve.tensor_copy(v_f[:, :, :], B[6][:, :].rearrange("p (a b) -> p a b", a=TOK)).then_inc(v_kept, 1)
            dve.wait_ge(norm_total, 3)
            dve.wait_ge(lat_lo, 1)
            dve.memset(va_hi[:, :, 0, 64:128].bitcast(F32), 0.0)
            dve.memset(va_hi[:, :, 1, 0:64].bitcast(F32), 0.0)
            dve.memset(va_lo[:, :, 0, 64:128].bitcast(F32), 0.0)
            dve.memset(va_lo[:, :, 1, 0:64].bitcast(F32), 0.0)
            dve.memset(pa[:, :, :, :], 0.0).then_inc(a_zeroed, 1)
            for m in range(A_TILES):
                dve.wait_ge(proj_done, T_QA + 1 + m)
                dve.wait_ge(rotated, 1 + m)
                rotate_terms(B[m], cos_r, sin_r, T_QA + 1 + m)
                dve.tensor_tensor(mixed[:, m, :], t1[:, :], t2[:, :], ALU.add).then_inc(rotated, 1)
            dve.wait_ge(proj_done, T_KR + 1)
            dve.wait_ge(rotated, 9)
            rotate_terms(B[3], cos_r, sin_r, T_KR + 1)
            dve.wait_ge(lat_scaled, 2)
            dve.tensor_tensor(t3[:, :], t1[:, :], t2[:, :], ALU.add).then_inc(rotated, 1)

            def a_maxima(t, u):
                i, m, slot = u // 2, u % 2, u % 2
                w = 2 * CHUNK if i == 0 else 3 * CHUNK
                st = st_a[:, slot, :, :]
                hd = bass.ds(4 * t + 2 * m, 2)
                dve.wait_ge(a_scores, A_UNITS * t + u + 1)
                dve.reduce_max(st[:, 0, :], B[4 + slot][:, 0:384].rearrange("p (a b) -> p a b", a=2)[:, :, 192 - w:192], AX.X).then_inc(a_max, 1)
                dve.wait_ge(a_max, 2 * (A_UNITS * t + u) + 1)
                dve.scalar_tensor_tensor(out=st[:, 1, :], in0=st[:, 0, :], scalar=-A_SCALE, op0=ALU.mult,
                                         in1=neg_sinks[:, hd], op1=ALU.min).then_inc(a_max, 1)
                dve.wait_ge(a_max, 2 * (A_UNITS * t + u) + 2)
                dve.tensor_tensor(st[:, 2, :], st[:, 1, :], sinks[:, hd], ALU.add).then_inc(a_shift, 1)

            def a_normalise(t, u):
                slot = u % 2
                st = st_a[:, slot, :, :]
                dve.wait_ge(a_exp, A_UNITS * t + u + 3)
                dve.tensor_tensor(st[:, 5, :], st[:, 3, :], st[:, 4, :], ALU.add).then_inc(a_recip, 1)
                dve.wait_ge(a_recip, 2 * (A_UNITS * t + u) + 1)
                dve.reciprocal(st[:, 5, :], st[:, 5, :]).then_inc(a_recip, 1)
                dve.wait_ge(a_recip, 2 * (A_UNITS * t + u) + 2)
                for e in range(2):
                    ins = dve.tensor_scalar(pa[:, slot, e, CHUNK:], pa[:, slot, e, CHUNK:], st[:, 5, e:e + 1], None, ALU.mult)
                ins.then_inc(a_probs, 1)

            def a_pt_low(t, u):
                i, m = u // 2, u % 2
                dve.wait_ge(a_pt_hi, A_UNITS * t + u + 1)
                ins = dve.tensor_tensor(pta_lo[:, m, 0:256], B[6][:, 0:256], pta_hi[:, m, 0:256].bitcast(F32), ALU.subtract)
                if i > 0:
                    ins = dve.tensor_tensor(pta_lo[:, m, 256:384].rearrange("p (a b) -> p a b", a=2),
                                            B[6][:, 256:512].rearrange("p (a b) -> p a b", a=2)[:, :, 0:64],
                                            pta_hi[:, m, 256:384].bitcast(F32).rearrange("p (a b) -> p a b", a=2), ALU.subtract)
                ins.then_inc(a_pt_lo, 1)

            dve.wait_ge(rotated, 10)
            dve.wait_ge(lat_hi, 2)
            dve.tensor_tensor(kr_lo[:, :], t3[:, :], kr_hi[:, :].bitcast(F32), ALU.subtract).then_inc(lat_lo, 1)
            with dve.Fori(0, 4) as t:
                dve.wait_ge(a_split_hi, 2 * t + 1)
                dve.tensor_tensor(qs[64:128, :, 0, :], mixed[0:64, bass.ds(2 * t, 2), :], qs[0:64, :, 0, :].bitcast(F32), ALU.subtract)
                dve.tensor_tensor(qs[0:64, :, 1, :], mixed[64:128, bass.ds(2 * t, 2), :], qs[64:128, :, 1, :].bitcast(F32), ALU.subtract)
                dve.wait_ge(a_split_hi, 2 * t + 2)
                g = t // 2
                dve.tensor_tensor(ks_lo[:, :], k_dup[:, bass.ds(g, 1), :].rearrange("p a b -> p (a b)"), ks_hi[:, :].bitcast(F32), ALU.subtract)
                for e in range(2):
                    ins = dve.tensor_tensor(va_lo[:, :, e, 64 * e:64 * e + 64], v_f[:, :, bass.ds(64 * g, 64)],
                                            va_hi[:, :, e, 64 * e:64 * e + 64].bitcast(F32), ALU.subtract)
                ins.then_inc(a_split_lo, 1)
                last = None
                for hf in range(17):
                    if last is not None:
                        a_normalise(t, last)
                        last = None
                    if hf in AT_SCORES:
                        a_maxima(t, AT_SCORES[hf])
                        last = AT_SCORES[hf]
                    if hf in AT_TRANSPOSE:
                        a_pt_low(t, AT_TRANSPOSE[hf])
                    if hf in AT_PV:
                        i = AT_PV[hf]
                        dve.wait_ge(a_pv, TOK * t + i + 2)
                        dve.tensor_scalar(mixed[:, bass.ds(2 * t, 2), P * i:P * i + P], B[7][:, 0:256].rearrange("p (a b) -> p a b", a=2),
                                          1.0, None, ALU.mult).then_inc(a_out, 1)
                for ct in range(4):
                    dve.wait_ge(proj_done, 4 * t + (T_GT + ct + 1))
                    dst = gate_tmp[:, ct, :] if ct < 2 else mixed[:, bass.ds(2 * t + (A_TILES + ct - 2), 1), :].rearrange("p a b -> p (a b)")
                    dve.tensor_tensor(dst, B[ct][:, :], rstd[:, :], ALU.mult).then_inc(proj_evac, 1)
                dve.wait_ge(a_out, TOK * t + 5)
                for ct in range(2):
                    dve.wait_ge(gate_silu, 4 * t + (ct + 1))
                    m = mixed[:, bass.ds(2 * t + ct, 1), :].rearrange("p a b -> p (a b)")
                    dve.tensor_tensor(m, m, gate_tmp[:, ct, :], ALU.mult).then_inc(gated, 1)
                dve.wait_ge(gated, 2 * t + 2)

            for k in range(CQ_T):
                dve.wait_ge(lat_hi, 3 + k)
                dve.tensor_tensor(cqs_lo[:, k, :], cq[:, k, :], cqs_hi[:, k, :].bitcast(F32), ALU.subtract).then_inc(lat_lo, 1)
            dve.wait_ge(rot_landed, 32)
            dve.wait_ge(gate_silu, 16)

            def b_tile_low(idx):
                p, j = divmod(idx, PB_TILES)
                par, bk = p % 2, B[idx % 4]
                if j == 4:
                    dve.wait_ge(proj_done, T_PB + idx + 1)
                    if p > 0:
                        dve.wait_ge(b_lo, p)
                    rotate_terms(bk, cos_b, sin_b, T_PB + idx + 1)
                    dve.tensor_tensor(t3[:, :], t1[:, :], t2[:, :], ALU.add).then_inc(b_rot, 1)
                    dve.wait_ge(b_rot, p + 1)
                    return
                dve.wait_ge(b_hi, idx + 1)
                if j in (1, 2):
                    dst, hi, src = vb_lo[par][:, 2 * j - 2:2 * j, :], vb_hi[par][:, 2 * j - 2:2 * j, :], bk[:, :].rearrange("p (a b) -> p a b", a=2)
                else:
                    h = {0: 0, 3: 1, 5: 0, 6: 1}[j]
                    dst, hi = (kn_lo, kn_hi) if j in (0, 3) else (qn_lo, qn_hi)
                    dst, hi, src = dst[par][:, h, :], hi[par][:, h, :], bk[:, :]
                dve.tensor_tensor(dst, src, hi.bitcast(F32), ALU.subtract).then_inc(proj_evac, 1)

            def b_rotary_low(p):
                par = p % 2
                dve.wait_ge(b_hi, PB_TILES * p + 5)
                dve.tensor_tensor(qr[par][64:128, 0, :], t3[0:64, :], qr[par][0:64, 0, :].bitcast(F32), ALU.subtract)
                dve.tensor_tensor(qr[par][0:64, 1, :], t3[64:128, :], qr[par][64:128, 1, :].bitcast(F32), ALU.subtract).then_inc(b_lo, 1)

            def b_maxima(w):
                u = w % 8
                n = P * (u % 4 + 1)
                dve.wait_ge(b_scores, w + 1)
                dve.reduce_max(st_b[:, u % 4, 0:1], B[4 + u % 2][:, 0:n], AX.X).then_inc(b_max, 1)
                dve.wait_ge(b_max, w + 1)
                dve.tensor_scalar(st_b[:, u % 4, 1:2], st_b[:, u % 4, 0:1], -B_SCALE, None, ALU.mult).then_inc(b_shift, 1)

            def b_normalise(w):
                u = w % 8
                n = P * (u % 4 + 1)
                dve.wait_ge(b_exp, w + 3)
                dve.reciprocal(st_b[:, u % 4, 3:4], st_b[:, u % 4, 2:3]).then_inc(b_recip, 1)
                dve.wait_ge(b_recip, w + 1)
                dve.tensor_scalar(pb[:, u % 4, 0:n], pb[:, u % 4, 0:n], st_b[:, u % 4, 3:4], None, ALU.mult).then_inc(b_probs, 1)

            def b_pt_low(w):
                i = w % 4
                dve.wait_ge(b_pt_hi, w + 1)
                dve.tensor_tensor(ptb_lo[:, 0:i + 1, P * i:P * i + P], B[6][:, 0:P * (i + 1)].rearrange("p (a b) -> p a b", a=i + 1),
                                  ptb_hi[:, 0:i + 1, P * i:P * i + P].bitcast(F32), ALU.subtract).then_inc(b_pt_lo, 1)

            def b_take(head):
                dve.wait_ge(b_pv, head + 2)
                m = mixed[:, A_TILES + head, :]
                dve.tensor_tensor(m, B[7][:, :], m, ALU.mult).then_inc(b_out, 1)

            def mixed_low(j):
                dve.wait_ge(m_hi, j + 1)
                dve.tensor_tensor(mx_lo[j][:, :, :], mixed[:, 2 * j:2 * j + 2, :], mx_hi[j][:, :, :].bitcast(F32), ALU.subtract).then_inc(m_lo, 1)

            for j in range(PB_TILES):
                b_tile_low(j)
                if j == 5:
                    b_rotary_low(0)
            for p in range(PAIRS):
                f, late = 0, None
                for step in B_STEPS:
                    w = 8 * p + (int(step[1]) if step[0] in "ST" else 0)
                    if step[0] == "S":
                        if late is not None:
                            b_normalise(late)
                        b_maxima(w)
                        late = w
                        continue
                    if step[0] == "T":
                        if late is not None:
                            b_normalise(late)
                            late = None
                        b_pt_low(w)
                    elif step[0] == "V":
                        b_take(2 * p + int(step[1]))
                    else:
                        if p < PAIRS - 1:
                            for j, ks in B_PIECES[f]:
                                if ks[-1] == (1 if j < 4 else 3):
                                    b_tile_low(PB_TILES * (p + 1) + j)
                                    if j == 5:
                                        b_rotary_low(p + 1)
                        elif f < 7:
                            mixed_low(f)
                        f += 1
                    if late is not None:
                        b_normalise(late)
                        late = None

            mixed_low(7)
            dve.wait_ge(y0_landed, 16)

            def residual(n, t):
                dve.wait_ge(o_done, 4 * n + (t + 1))
                ys = y[:, t, bass.ds(SEQ * n, SEQ)]
                dve.tensor_tensor(ys, B[t][:, :], ys, ALU.add).then_inc(o_evac, 1)

            for t in range(TOK):
                residual(0, t)
            dve.wait_ge(y_landed, 64)
            with dve.Fori(1, 3) as n:
                for t in range(TOK):
                    residual(n, t)
            for t in range(TOK):
                residual(3, t)
                dve.wait_ge(o_squared, 12 + t + 2)
                dve.reduce_sum(fin[:, t, 0:1], sumsq[:, t, :], AX.X).then_inc(o_sum, 1)
                dve.wait_ge(o_root, t + 1)
                dve.reciprocal(fin[:, t, 2:3], fin[:, t, 1:2]).then_inc(o_recip, 1)
                dve.wait_ge(o_recip, t + 1)
                ys = y[:, t, 3 * SEQ:]
                dve.scalar_tensor_tensor(out=ys, in0=ys, scalar=fin[:, t, 2:3], op0=ALU.mult, in1=fw[:, 3 * SEQ:], op1=ALU.mult)
                dve.wait_ge(o_gained, 12)
                ys = y[:, t, 2 * SEQ:3 * SEQ]
                dve.tensor_scalar(ys, ys, fin[:, t, 2:3], None, ALU.mult).then_inc(o_scaled, 1)

        @block.tensor
        def _(pe):
            def three(dst, ah, al, bh, bl, start, stop, frees_chunk=False):
                ins = pe.matmul(dst, ah, bh, start=start, stop=False)
                if frees_chunk:
                    ins.then_inc(w_used, 1)
                pe.matmul(dst, al, bh, start=False, stop=False)
                return pe.matmul(dst, ah, bl, start=False, stop=stop)

            def columns(s, banks, tiles, ks, frees_chunk, width=SEQ):
                for ct in tiles:
                    for n, k in enumerate(ks):
                        o = width * n + P * ct
                        ins = three(B[banks[ct]][:, :], w_hi[:, s % HL, o:o + P], w_lo[:, s % HL, o:o + P],
                                    x_hi[:, k, :], x_lo[:, k, :], k == 0, k == K_IN - 1, frees_chunk and ct == tiles[0] and n == 0)
                    if ks[-1] == K_IN - 1:
                        ins.then_inc(proj_done, 1)

            def group(c0, banks, free=None, with_x=False):
                for s in range(8):
                    pe.wait_ge(w_lo_ready, c0 + s + 1)
                    if with_x:
                        pe.wait_ge(x_lo_ready, s + 1)
                    for ct in range(4):
                        if s == 0 and free is not None:
                            pe.wait_ge(proj_evac, free + ct)
                        columns(c0 + s, banks, (ct,), (2 * s, 2 * s + 1), ct == 0 and c0 + s > 0)

            pe.sem_inc(a_turned, 2)
            pe.sem_inc(a_pv, 1)
            pe.sem_inc(b_turned, 4)
            pe.sem_inc(b_pv, 1)
            group(KV0, (0, 1, 2, 3), with_x=True)
            pe.wait_ge(consts_set, 2)
            pe.wait_ge(norm_sum, 1)
            pe.matmul(B[7][:, :], ones[:, :], t1[:, :], start=True, stop=True).then_inc(norm_total, 1)
            for s in range(8):
                pe.wait_ge(w_lo_ready, CQ0 + s + 1)
                for ct in range(4):
                    if s == 0 and ct == 3:
                        pe.wait_ge(norm_root, 1)
                    columns(CQ0 + s, (4, 5, 6, 7), (ct,), (2 * s, 2 * s + 1), ct == 0)
            for s in range(16):
                first = s < 8
                pe.wait_ge(w_lo_ready, QA0 + s + 1)
                for ct in range(4):
                    if s == 0:
                        pe.wait_ge(proj_evac, ct + 1)
                    if s == 8 and ct == 0:
                        pe.wait_ge(norm_root, 3)
                        pe.wait_ge(v_kept, 1)
                    columns(QA0 + s, (0, 1, 2, 3) if first else (4, 5, 6, 7), (ct,), (2 * (s % 8), 2 * (s % 8) + 1), ct == 0)
                if s == 3:
                    pe.wait_ge(proj_evac, T_QA)
                    pe.wait_ge(tables_landed, 48)
                    for t in range(TOK):
                        ins = pe.transpose(B[6][:, P * t:P * t + P], v_t[:, P * t:P * t + P], ident[:, :])
                    ins.then_inc(v_turned, 1)
                    pe.wait_ge(norm_sum, 2)
                    pe.matmul(B[4][:, :], ones[:, :], t3[:, :], start=True, stop=True).then_inc(norm_total, 1)
                    pe.wait_ge(norm_sum, 3)
                    pe.matmul(B[5][:, :], ones[:, :], sq[:, 0, 0:SEQ], start=True, stop=True).then_inc(norm_total, 1)
            pe.wait_ge(proj_evac, T_QA + 4)
            for s in range(2):
                pe.wait_ge(w_lo_ready, KR0 + s + 1)
                columns(KR0 + s, (3,), (0,), tuple(range(8 * s, 8 * s + 8)), True, width=P)

            def a_score(t, u):
                i, m, slot = u // 2, u % 2, u % 2
                w = 2 * CHUNK if i == 0 else 3 * CHUNK
                pe.wait_ge(a_exp, A_UNITS * t + u + 1)
                k0 = P * (i + 1) - w
                for e in range(2):
                    dst = B[4 + slot][:, 192 * e + 192 - w:192 * e + 192]
                    q = qs[:, m, e, P * i:P * i + P]
                    pe.matmul(dst, q, ks_hi[:, k0:k0 + w], start=e == 0, stop=False)
                    pe.matmul(dst, q, ks_lo[:, k0:k0 + w], start=False, stop=False)
                both = B[4 + slot][:, 0:384].rearrange("p (a b) -> p a b", a=2)
                if i > 0:
                    pe.matmul(both[:, :, 0:CHUNK], ident_bf[:, :], mask_bf[:, 0, :, :], start=False, stop=False)
                pe.matmul(both[:, :, 2 * CHUNK:3 * CHUNK], ident_bf[:, :], mask_bf[:, 1, :, :], start=False, stop=True).then_inc(a_scores, 1)

            def a_transpose(t, u):
                i, slot = u // 2, u % 2
                pe.wait_ge(a_probs, A_UNITS * t + u + 1)
                pe.wait_ge(a_pt_lo, A_UNITS * t + u + 1)
                for e in range(2):
                    ins = pe.transpose(B[6][:, P * e:P * e + P], pa[:, slot, e, 2 * CHUNK:], ident[:, :])
                if i > 0:
                    for e in range(2):
                        ins = pe.transpose(B[6][:, 256 + P * e:256 + P * e + P], pa[:, slot, e, 0:2 * CHUNK], ident[:, :])
                ins.then_inc(a_turned, 1)

            def a_product(t, i):
                pe.wait_ge(a_pt_lo, A_UNITS * t + 2 * i + 3)
                pe.wait_ge(a_out, TOK * t + i + 1)
                dst = B[7][:, 0:256].rearrange("p (a b) -> p a b", a=2)
                for e in range(2):
                    ins = three(dst, va_hi[:, i, e, :], va_lo[:, i, e, :], pta_hi[:, :, P * e:P * e + P], pta_lo[:, :, P * e:P * e + P],
                                e == 0, i == 0 and e == 1)
                if i > 0:
                    for e in range(2):
                        o = 256 + CHUNK * e
                        ins = three(dst[:, :, 0:CHUNK], va_hi[:, i - 1, e, :], va_lo[:, i - 1, e, :],
                                    pta_hi[:, :, o:o + CHUNK], pta_lo[:, :, o:o + CHUNK], False, e == 1)
                ins.then_inc(a_pv, 1)

            pe.wait_ge(consts_set, 6)
            with pe.Fori(0, 4) as t:
                for hf in range(16):
                    if hf in AT_PV:
                        a_product(t, AT_PV[hf])
                    if hf in AT_TRANSPOSE:
                        a_transpose(t, AT_TRANSPOSE[hf])
                    if hf in AT_SCORES:
                        if AT_SCORES[hf] == 0:
                            pe.wait_ge(proj_evac, T_GT)
                            pe.wait_ge(a_split_lo, t + 1)
                        a_score(t, AT_SCORES[hf])
                    s = hf // 2
                    if hf % 2 == 0:
                        pe.wait_ge(w_lo_ready, 8 * t + (GT0 + s + 1))
                    for ct in (0, 1) if hf % 2 == 0 else (2, 3):
                        if s == 0:
                            pe.wait_ge(proj_evac, 4 * t + (T_GT - 4 + ct + 1))
                        columns(GT0 + s, (0, 1, 2, 3), (ct,), (2 * s, 2 * s + 1), ct == 0)
                a_product(t, AT_PV[16])

            def b_project(p, j, ks):
                idx = PB_TILES * p + j
                bk = B[idx % 4]
                c = PB0 + 3 * p + CHUNK_OF_TILE[j]
                slot = c % HL
                last = ks[-1] == (CKV_T if j < 4 else CQ_T) - 1
                if ks[0] == 0:
                    pe.wait_ge(proj_evac, T_PB + idx - 3)
                    pe.wait_ge(w_lo_ready, c + 1)
                    if j == 4:
                        pe.wait_ge(lat_lo, 2 + CQ_T)
                if j in (1, 2):
                    for tt in range(2):
                        tok = 2 * (j - 1) + tt
                        for k in ks:
                            o = 512 + 256 * k
                            ins = three(bk[:, 256 * tt:256 * tt + 256], ckv_hi[:, k, P * tok:P * tok + P], ckv_lo[:, k, P * tok:P * tok + P],
                                        w_hi[:, slot, o:o + 256], w_lo[:, slot, o:o + 256], k == 0, k == CKV_T - 1)
                else:
                    rhs_hi, rhs_lo = (ckv_hi, ckv_lo) if j < 4 else (cqs_hi, cqs_lo)
                    step = P if j == 4 else 2 * P
                    for k in ks:
                        o = step * k + (P if j in (3, 6) else 0)
                        ins = three(bk[:, :], w_hi[:, slot, o:o + P], w_lo[:, slot, o:o + P], rhs_hi[:, k, :], rhs_lo[:, k, :],
                                    k == 0, last and k == ks[-1], k == 0 and j in (0, 4, 5))
                if last:
                    ins.then_inc(proj_done, 1)

            def b_score(w):
                h, i, par = w % 8 // 4, w % 4, w // 8 % 2
                n = P * (i + 1)
                pe.wait_ge(b_exp, w + 1)
                dst = B[4 + w % 2][:, 0:n]
                q = slice(P * i, P * i + P)
                pe.matmul(dst, qr[par][:, h, q], kr_hi[:, 0:n], start=True, stop=False)
                pe.matmul(dst, qr[par][:, h, q], kr_lo[:, 0:n], start=False, stop=False)
                three(dst, qn_hi[par][:, h, q], qn_lo[par][:, h, q], kn_hi[par][:, h, 0:n], kn_lo[par][:, h, 0:n], False, False)
                pe.matmul(B[4 + w % 2][:, n - CHUNK:n], ident_bf[:, :], mask_bf[:, 1, 0, :], start=False, stop=True).then_inc(b_scores, 1)

            def b_transpose(w):
                pe.wait_ge(b_probs, w + 1)
                pe.wait_ge(b_pt_lo, w + 1)
                for kt in range(w % 4 + 1):
                    ins = pe.transpose(B[6][:, P * kt:P * kt + P], pb[:, w % 4, P * kt:P * kt + P], ident[:, :])
                ins.then_inc(b_turned, 1)

            def b_product(head):
                h, par = head % 2, head // 2 % 2
                pe.wait_ge(b_pt_lo, 4 * head + 5)
                pe.wait_ge(b_out, head + 1)
                for kt in range(TOK):
                    v = slice(P * h, P * h + P)
                    ins = three(B[7][:, P * kt:SEQ], vb_hi[par][:, kt, v], vb_lo[par][:, kt, v],
                                ptb_hi[:, kt, P * kt:SEQ], ptb_lo[:, kt, P * kt:SEQ], kt == 0, kt == TOK - 1)
                ins.then_inc(b_pv, 1)

            def out_rows(n, s, t, frees_chunk):
                slot = (WO0 + s) % HL
                for kk in range(2):
                    ins = three(B[t][:, :], mx_hi[s][:, kk, P * t:P * t + P], mx_lo[s][:, kk, P * t:P * t + P],
                                w_hi[:, slot, SEQ * kk:SEQ * kk + SEQ], w_lo[:, slot, SEQ * kk:SEQ * kk + SEQ],
                                s == 0 and kk == 0, s == 7 and kk == 1, frees_chunk and kk == 0)
                if s == 7:
                    ins.then_inc(o_done, 1)

            for j in range(PB_TILES):
                b_project(0, j, (0, 1) if j < 4 else (0, 1, 2, 3))
            pe.wait_ge(a_out, 17)
            for p in range(PAIRS):
                pe.wait_ge(proj_evac, T_PB + PB_TILES * (p + 1))
                pe.wait_ge(b_lo, p + 1)
                f = 0
                for step in B_STEPS:
                    if step[0] == "S":
                        b_score(8 * p + int(step[1]))
                    elif step[0] == "T":
                        b_transpose(8 * p + int(step[1]))
                    elif step[0] == "V":
                        b_product(2 * p + int(step[1]))
                    else:
                        if p < PAIRS - 1:
                            for j, ks in B_PIECES[f]:
                                b_project(p + 1, j, ks)
                        else:
                            done = sum(OUT_PIECES[:f])
                            for piece in range(done, done + OUT_PIECES[f]):
                                s, t = divmod(piece, 4)
                                if t == 0:
                                    pe.wait_ge(w_lo_ready, WO0 + s + 1)
                                    pe.wait_ge(m_lo, s + 1)
                                out_rows(0, s, t, t == 0)
                        f += 1

            def out_chunks(n, chunks):
                for s in chunks:
                    pe.wait_ge(w_lo_ready, 8 * n + (WO0 + s + 1))
                    pe.wait_ge(m_lo, s + 1)
                    for t in range(TOK):
                        if s == 0:
                            pe.wait_ge(o_evac, 4 * n + (t + 1))
                        out_rows(n, s, t, t == 0)

            out_chunks(0, range(4, 8))
            with pe.Fori(1, 3) as n:
                out_chunks(n, range(8))
            out_chunks(3, range(4))
            for t in range(TOK):
                for s in range(4, 8):
                    if t == 0:
                        pe.wait_ge(w_lo_ready, WO0 + 24 + s + 1)
                    out_rows(3, s, t, t == 0 and s == 4)


def laid_out_weights(w_in, w_q_b, w_kv_b, w_out):
    def cols(*parts):
        return np.concatenate(parts, axis=1)

    def chunked(w, ks):
        k, c = w.shape
        return w.reshape(k // (P * ks), ks, P, c).transpose(0, 2, 1, 3).reshape(-1, P, ks * c)

    a_w, kv_w = A_HEADS * A_DIM, A_KV_HEADS * A_DIM
    o = np.cumsum([0, a_w, kv_w, kv_w, a_w, Q_LORA, KV_LORA, B_ROPE, B_HEADS * B_V])
    a_q, a_k, a_v, a_g, b_cq, b_ckv, b_kr, b_g = (w_in[:, o[i]:o[i + 1]] for i in range(8))
    stream = [chunked(cols(a_k, a_v, b_ckv), 2), chunked(b_cq, 2), chunked(a_q[:, 0:SEQ], 2), chunked(a_q[:, SEQ:], 2),
              chunked(cols(b_kr, b_kr), 8)]
    for t in range(4):
        c = slice(2 * P * t, 2 * P * t + 2 * P)
        stream.append(chunked(cols(a_g[:, c], b_g[:, c]), 2))
    q = w_q_b.reshape(Q_LORA, B_HEADS, B_NOPE + B_ROPE)
    kv = w_kv_b.reshape(KV_LORA, B_HEADS, B_NOPE + B_V)
    pad = np.zeros((1, P, CE // 2), w_q_b.dtype)
    for p in range(B_HEADS // 2):
        h = slice(2 * p, 2 * p + 2)
        kn = chunked(kv[:, h, :B_NOPE].reshape(KV_LORA, -1), 2)
        v = chunked(kv[:, h, B_NOPE:].reshape(KV_LORA, -1), 2)
        qn = chunked(q[:, h, :B_NOPE].reshape(Q_LORA, -1), 4)
        qr = chunked(q[:, h, B_NOPE:].reshape(Q_LORA, -1), 4)
        stream += [np.concatenate([kn, v], axis=2), np.concatenate([qr, pad], axis=2), qn]
    for n in range(4):
        stream.append(chunked(w_out[:, SEQ * n:SEQ * n + SEQ], 2))
    stream = np.concatenate(stream, axis=0)
    assert stream.shape == (CHUNKS, P, CE)
    return np.ascontiguousarray(stream)


def rotary_tables():
    half = A_DIM // 2
    inv_freq = np.float32(1) / (np.float32(10000.0) ** (np.arange(0, A_DIM, 2, dtype=np.float32) / np.float32(A_DIM)))
    ang = np.arange(SEQ, dtype=np.float32)[None, :] * inv_freq.astype(np.float32)[:, None]
    cos, sin = np.cos(ang.astype(np.float64)), np.sin(ang.astype(np.float64))
    assert half == 32 and A_DIM == B_ROPE
    cos = np.concatenate([cos] * 4, axis=0)
    sin = np.concatenate([-sin, sin] * 2, axis=0)
    return np.ascontiguousarray(np.concatenate([np.eye(P), cos, sin], axis=1).astype(np.float32))


def kernel(x, norm_in_w, w_in, sinks_a, q_a_norm_w, w_q_b, kv_a_norm_w, w_kv_b, w_out, final_norm_w):
    import concourse.bacc as bacc
    from concourse.bass_utils import run_bass_kernel_spmd

    x, norm_in_w, w_in, sinks_a, q_a_norm_w, w_q_b, kv_a_norm_w, w_kv_b, w_out, final_norm_w = (
        np.asarray(a) for a in (x, norm_in_w, w_in, sinks_a, q_a_norm_w, w_q_b, kv_a_norm_w, w_kv_b, w_out, final_norm_w))
    arrays = {
        "w_stream": laid_out_weights(w_in, w_q_b, w_kv_b, w_out),
        "x_t": np.ascontiguousarray(x[0].T.reshape(8, 2, P, SEQ).transpose(0, 2, 1, 3).reshape(8, P, CE)),
        "x_nat": np.ascontiguousarray(x),
        "gains": np.ascontiguousarray(np.concatenate(
            [norm_in_w.reshape(K_IN, P).T, q_a_norm_w.reshape(CQ_T, P).T, kv_a_norm_w.reshape(CKV_T, P).T,
             np.broadcast_to(sinks_a[None, :], (P, A_HEADS))], axis=1)),
        "final_w": np.ascontiguousarray(np.broadcast_to(final_norm_w[None, :], (P, D_MODEL))),
        "tables": rotary_tables(),
    }
    nc = bacc.Bacc("TRN2", target_bir_lowering=False, num_devices=1)
    args = [nc.dram_tensor(name, a.shape, mybir.dt.from_np(a.dtype), kind="ExternalInput").ap() for name, a in arrays.items()]
    args.append(nc.dram_tensor("out", (1, SEQ, D_MODEL), F32, kind="ExternalOutput").ap())
    build(nc, *args)
    r = run_bass_kernel_spmd(nc, [arrays], core_ids=[0])
    return r.results[0]["out"]
```

```python
from contextlib import ExitStack

import concourse.bass as bass
import numpy as np
from concourse import mybir

ALU = mybir.AluOpType
ACT = mybir.ActivationFunctionType
AX = mybir.AxisListType
F32 = mybir.dt.float32
F32R = mybir.dt.float32r
BF16 = mybir.dt.bfloat16

P = 128
D_MODEL, SEQ = 2048, 512
CHUNK = 64
EPS = 1e-6
MASK_VALUE = -1e30
A_HEADS, A_KV_HEADS, A_DIM = 16, 2, 64
B_HEADS, B_NOPE, B_ROPE, B_V = 8, 128, 64, 128
Q_LORA, KV_LORA = 512, 256
A_SCALE = A_DIM ** -0.5
B_SCALE = (B_NOPE + B_ROPE) ** -0.5
K_IN = D_MODEL // P
TOK = SEQ // P
A_TILES = A_HEADS * A_DIM // P
B_TILES = B_HEADS * B_V // P
MIX_TILES = A_TILES + B_TILES
CQ_T, CKV_T = Q_LORA // P, KV_LORA // P

CE = 1024
KV0 = 0
CQ0 = KV0 + 8
QA0 = CQ0 + 8
KR0 = QA0 + 16
GT0 = KR0 + 2
PB0 = GT0 + 32
WO0 = PB0 + 12
CHUNKS = WO0 + 32
RAW, HL = 2, 4
AHEAD = 3

T_CQ, T_QA, T_KR, T_GT = 4, 8, 16, 17
T_PB = T_GT + 16
PAIRS = B_HEADS // 2
PB_TILES = 7

A_UNITS = 8
AT_SCORES = {4: 0, 5: 1, 7: 2, 8: 3, 9: 4, 11: 5, 12: 6, 13: 7}
AT_TRANSPOSE = {6: 0, 7: 1, 9: 2, 10: 3, 11: 4, 13: 5, 14: 6, 15: 7}
AT_PV = {8: 0, 11: 1, 14: 2, 16: 3}

B_STEPS = ("S0 F S1 L F S2 T0 F S3 T1 F S4 T2 F S5 T3 F S6 F V0 T4 S7 F T5 F T6 F T7 F").split()
B_PIECES = [((0, (0, 1)),), ((1, (0, 1)),), ((2, (0, 1)),), ((3, (0, 1)),), ((4, (0, 1)),), ((4, (2, 3)),), ((5, (0, 1)),),
            ((5, (2, 3)),), ((6, (0, 1)),), ((6, (2, 3)),), ()]
CHUNK_OF_TILE = (0, 0, 0, 0, 1, 2, 2)
SPLIT = {0: 0, 1: 1, 2: 2, 3: 3, 5: 4, 6: 5}
B_SPLITS = {1: 0, 2: 1, 3: 2, 4: 3, 8: 5, 10: 6}
B_CHUNKS = {0: 0, 5: 1, 6: 2}
B_ROTARY = {6: 0, 7: 1}
M_AT = {1: 1, 2: 2, 4: 3, 5: 4, 7: 5, 9: 6}
OUT_PIECES = [2, 1, 1, 1, 1, 1, 2, 2, 2, 1, 2]


def build(nc, w_stream, x_t, x_nat, gains, final_w, tables, out):
    with ExitStack() as ctx:
        def sem(name):
            return ctx.enter_context(nc.semaphore(name))

        def bank(name):
            return ctx.enter_context(nc.psum_tensor(name, [P, 512], F32))

        base = (nc.sbuf_base + 31) // 32 * 32
        place = [base]

        def at(name, shape, dt, offset):
            return nc.alloc_sbuf_tensor_at(name, shape, dt, offset=offset)

        def region(nbytes):
            start = place[0]
            place[0] += (nbytes + 31) // 32 * 32
            return start

        r_x = region(2 * K_IN * SEQ * 4)
        x_hi = at("x_hi", [P, K_IN, SEQ], F32R, r_x)
        x_lo = at("x_lo", [P, K_IN, SEQ], F32R, r_x + K_IN * SEQ * 4)
        KB = 1024
        cqs_hi = at("cqs_hi", [P, CQ_T, SEQ], F32R, r_x + 32 * KB)
        cqs_lo = at("cqs_lo", [P, CQ_T, SEQ], F32R, r_x + 40 * KB)
        ptb_hi = at("ptb_hi", [P, TOK, SEQ], F32R, r_x + 48 * KB)
        ptb_lo = at("ptb_lo", [P, TOK, SEQ], F32R, r_x + 56 * KB)

        b_tmp = at("b_tmp", [P, 2, SEQ], F32, r_x + 28 * KB)

        r_mixed = region(MIX_TILES * SEQ * 4)
        mixed = at("mixed", [P, MIX_TILES, SEQ], F32, r_mixed)

        w_raw = at("w_raw", [P, RAW, CE], F32, region(RAW * CE * 4))
        w_hi = at("w_hi", [P, HL, CE], F32R, region(HL * CE * 4))
        w_lo = at("w_lo", [P, HL, CE], F32R, region(HL * CE * 4))

        gain = at("gain", [P, 38], F32, region(38 * 4))
        g_in, g_q, g_kv, sinks = gain[:, 0:16], gain[:, 16:20], gain[:, 20:22], gain[:, 22:38]
        neg_sinks = at("neg_sinks", [P, A_HEADS], F32, region(64))
        eps = at("eps", [P, 1], F32, region(4))
        preloaded = at("preloaded", [P, 1], F32, region(4))
        ident = at("ident", [P, P], F32, region(512))
        ones = at("ones", [P, P], F32, region(512))
        ident_bf = at("ident_bf", [P, P], BF16, region(256))
        mask_bf = at("mask_bf", [P, 2, 2, CHUNK], BF16, region(512))
        st_a = at("st_a", [P, 2, 6, 2], F32, region(96))
        st_b = at("st_b", [P, 4, 4], F32, region(64))
        sumsq = at("sumsq", [P, TOK, 4], F32, region(64))
        fin = at("fin", [P, TOK, 3], F32, region(48))
        rstd = at("rstd", [P, SEQ], F32, region(2048))
        r_rot = region(4096)
        cos_r = at("cos_r", [P, SEQ], F32, r_rot)
        sin_r = at("sin_r", [P, SEQ], F32, r_rot + 2048)
        gate_tmp = at("gate_tmp", [P, 2, SEQ], F32, r_rot)
        cos_b = at("cos_b", [P, SEQ], F32, r_rot)
        sin_b = at("sin_b", [P, SEQ], F32, r_rot + 2048)
        r_ckv = region(8192)
        ckv_hi = at("ckv_hi", [P, CKV_T, SEQ], F32R, r_ckv)
        ckv_lo = at("ckv_lo", [P, CKV_T, SEQ], F32R, r_ckv + 4096)
        fw = at("fw", [P, D_MODEL], F32, r_ckv)
        r_cq = region(8192)
        cq = at("cq", [P, CQ_T, SEQ], F32, r_cq)
        kr_hi = at("kr_hi", [P, SEQ], F32R, region(2048))
        kr_lo = at("kr_lo", [P, SEQ], F32R, region(2048))
        r_tmp = region(6144)
        t1 = at("t1", [P, SEQ], F32, r_tmp)
        t2 = at("t2", [P, SEQ], F32, r_tmp + 2048)
        t3 = at("t3", [P, SEQ], F32, r_tmp + 4096)
        r4 = region(36 * KB)
        xs = at("xs", [P, 2, CE], F32, r4)
        sq = at("sq", [P, 2, CE], F32, r4 + 8 * KB)
        acc = at("acc", [P, CE], F32, r4 + 16 * KB)
        ckv = at("ckv", [P, CKV_T, SEQ], F32, r4 + 20 * KB)
        v_t = at("v_t", [P, SEQ], F32, r4 + 24 * KB)
        qs = at("qs", [P, 2, 2, SEQ], F32R, r4)
        ks_hi = at("ks_hi", [P, SEQ], F32R, r4 + 8 * KB)
        ks_lo = at("ks_lo", [P, SEQ], F32R, r4 + 10 * KB)
        va_hi = at("va_hi", [P, TOK, 2, P], F32R, r4 + 12 * KB)
        va_lo = at("va_lo", [P, TOK, 2, P], F32R, r4 + 16 * KB)
        pa = at("pa", [P, 2, 2, 4 * CHUNK], F32, r4 + 20 * KB)
        pta_hi = at("pta_hi", [P, 2, 384], F32R, r4 + 24 * KB)
        pta_lo = at("pta_lo", [P, 2, 384], F32R, r4 + 27 * KB)
        k_dup = at("k_dup", [P, A_KV_HEADS, SEQ], F32, r4 + 30 * KB)
        v_f = at("v_f", [P, TOK, P], F32, r4 + 34 * KB)
        qn_hi, qn_lo, kn_hi, kn_lo, qr, vb_hi, vb_lo = ([] for _ in range(7))
        for par, r in enumerate((r_x, r4)):
            for n, (kept, name) in enumerate(((qn_hi, "qn_hi"), (qn_lo, "qn_lo"), (kn_hi, "kn_hi"), (kn_lo, "kn_lo"), (qr, "qr"))):
                kept.append(at(f"{name}{par}", [P, 2, SEQ], F32R, r + 4 * KB * n))
            vb_hi.append(at(f"vb_hi{par}", [P, TOK, 2 * P], F32R, r + 20 * KB))
            vb_lo.append(at(f"vb_lo{par}", [P, TOK, 2 * P], F32R, r + 24 * KB))
        pb = at("pb", [P, 4, SEQ], F32, r4 + 28 * KB)
        m_at = [r_cq, r_x, r_x + 8 * KB, r_x + 16 * KB, r_x + 32 * KB, r_x + 40 * KB, r_x + 24 * KB, r_x + 48 * KB]
        mx_hi = [at(f"mx_hi{j}", [P, 2, SEQ], F32R, o) for j, o in enumerate(m_at)]
        mx_lo = [at(f"mx_lo{j}", [P, 2, SEQ], F32R, o + 4 * KB) for j, o in enumerate(m_at)]
        y = at("y", [P, TOK, D_MODEL], F32, r4)
        junk = at("junk", [P, SEQ], F32, r4 + 32 * KB)
        assert place[0] <= nc.sbuf_usable_end, place[0]

        B = [bank(f"bank{i}") for i in range(8)]

        w_landed = [sem(f"w_landed{i}") for i in range(RAW)]
        w_hi_ready, w_lo_ready, w_used = sem("w_hi_ready"), sem("w_lo_ready"), sem("w_used")
        x_landed = [sem("x_landed0"), sem("x_landed1")]
        x_hi_ready, x_lo_ready, x_squared, x_summed = sem("x_hi_ready"), sem("x_lo_ready"), sem("x_squared"), sem("x_summed")
        gains_landed, tables_landed, rot_landed = sem("gains_landed"), sem("tables_landed"), sem("rot_landed")
        y0_landed, y_landed = sem("y0_landed"), sem("y_landed")
        consts_set = sem("consts_set")
        norm_sum, norm_total, norm_root, norm_recip = sem("norm_sum"), sem("norm_total"), sem("norm_root"), sem("norm_recip")
        proj_done, proj_evac, gate_evac = sem("proj_done"), sem("proj_evac"), sem("gate_evac")
        rotated, lat_scaled, lat_hi, lat_lo = sem("rotated"), sem("lat_scaled"), sem("lat_hi"), sem("lat_lo")
        v_turned, v_kept, squares = sem("v_turned"), sem("v_kept"), sem("squares")
        a_zeroed, a_split_hi, a_split_lo = sem("a_zeroed"), sem("a_split_hi"), sem("a_split_lo")
        a_scores, a_max, a_shift, a_exp, a_recip, a_probs = sem("a_scores"), sem("a_max"), sem("a_shift"), sem("a_exp"), sem("a_recip"), sem("a_probs")
        a_turned, a_pt_hi, a_pt_lo, a_pv, a_out = sem("a_turned"), sem("a_pt_hi"), sem("a_pt_lo"), sem("a_pv"), sem("a_out")
        gate_silu, gated = sem("gate_silu"), sem("gated")
        cqs_split, b_hi, b_lo = sem("cqs_split"), sem("b_hi"), sem("b_lo")
        b_rot_evac, b_rot, b_rot_hi, b_rot_lo = sem("b_rot_evac"), sem("b_rot"), sem("b_rot_hi"), sem("b_rot_lo")
        b_scores, b_max, b_exp, b_recip, b_probs = sem("b_scores"), sem("b_max"), sem("b_exp"), sem("b_recip"), sem("b_probs")
        b_turned, b_pt_hi, b_pt_lo, b_pv, b_out = sem("b_turned"), sem("b_pt_hi"), sem("b_pt_lo"), sem("b_pv"), sem("b_out")
        m_hi, m_lo, m_lo_pool = sem("m_hi"), sem("m_lo"), sem("m_lo_pool")
        o_done, o_evac, o_squared, o_gained, o_sum, o_root = sem("o_done"), sem("o_evac"), sem("o_squared"), sem("o_gained"), sem("o_sum"), sem("o_root")
        o_recip, o_scaled, o_scaled_act, stored = sem("o_recip"), sem("o_scaled"), sem("o_scaled_act"), sem("stored")

        block = ctx.enter_context(nc.Block())

        @block.sync
        def _(sp):
            for j in range(8):
                if j >= RAW:
                    sp.wait_ge(w_lo_ready, j - 1)
                sp.dma_start(w_raw[:, j % RAW, :], w_stream[j, :, :]).then_inc(w_landed[j % RAW], 16)
                if j >= 2:
                    sp.wait_ge(x_lo_ready, j - 1)
                    sp.wait_ge(x_squared, j - 1)
                sp.dma_start(xs[:, j % 2, :], x_t[j, :, :]).then_inc(x_landed[j % 2], 16)
            with sp.Fori(0, (CHUNKS - 8) // RAW) as i:
                for s in range(RAW):
                    sp.wait_ge(w_lo_ready, RAW * i + (7 + s))
                    sp.dma_start(w_raw[:, s, :], w_stream[bass.ds(RAW * i + (8 + s), 1), :, :].rearrange("a p c -> (a p) c"))\
                        .then_inc(w_landed[s], 16)
            for t in range(TOK):
                sp.wait_ge(o_scaled_act, t + 1)
                sp.dma_start(out[0, P * t:P * t + P, 0:CE], y[:, t, 0:CE]).then_inc(stored, 16)
                sp.wait_ge(o_scaled, t + 1)
                sp.dma_start(out[0, P * t:P * t + P, CE:], y[:, t, CE:]).then_inc(stored, 16)
            sp.wait_ge(stored, 16 * 2 * TOK)

        @block.gpsimd
        def _(pool):
            def low_part(c, s):
                pool.wait_ge(w_hi_ready, c + 1)
                pool.tensor_tensor(w_lo[:, s % HL, :], w_raw[:, s % RAW, :], w_hi[:, s % HL, :].bitcast(F32), ALU.subtract)\
                    .then_inc(w_lo_ready, 1)

            def b_tile_low(p, j):
                n, par = 6 * p + SPLIT[j], p % 2
                pool.wait_ge(b_hi, n + 1)
                src = b_tmp[:, n % 2, :]
                if j in (1, 2):
                    dst, hi = vb_lo[par][:, 2 * j - 2:2 * j, :], vb_hi[par][:, 2 * j - 2:2 * j, :]
                    src = src.rearrange("p (a b) -> p a b", a=2)
                else:
                    dst, hi = (kn_lo, kn_hi) if j in (0, 3) else (qn_lo, qn_hi)
                    dst, hi = dst[par][:, j in (3, 6), :], hi[par][:, j in (3, 6), :]
                pool.tensor_tensor(dst, src, hi.bitcast(F32), ALU.subtract).then_inc(b_lo, 1)

            def mixed_low(j):
                pool.wait_ge(m_hi, j + 1)
                if j == 6:
                    pool.wait_ge(b_lo, 6 * PAIRS)
                pool.tensor_tensor(mx_lo[j][:, :, :], mixed[:, 2 * j:2 * j + 2, :], mx_hi[j][:, :, :].bitcast(F32), ALU.subtract)\
                    .then_inc(m_lo_pool, 1)

            b_head = PB0 + AHEAD + 3
            pool.wait_ge(w_lo_ready, 1)
            for c in range(1, HL):
                low_part(c, c)
            with pool.Fori(1, b_head // HL) as i:
                for s in range(HL):
                    low_part(HL * i + s, s)
            for c in range(b_head // HL * HL, b_head):
                low_part(c, c)
            for p in range(PAIRS):
                for f in range(len(B_PIECES)):
                    if p < PAIRS - 1:
                        if f in B_SPLITS:
                            b_tile_low(p + 1, B_SPLITS[f])
                        if f in B_CHUNKS:
                            c = PB0 + 3 * (p + 1) + B_CHUNKS[f] + AHEAD
                            low_part(c, c)
                        if p == PAIRS - 2 and f == 6:
                            mixed_low(0)
                    else:
                        if f in M_AT:
                            mixed_low(M_AT[f])
                        done = sum(OUT_PIECES[:f])
                        for piece in range(done, done + OUT_PIECES[f]):
                            if piece % 4 == 0:
                                c = WO0 + piece // 4 + AHEAD
                                low_part(c, c)
            head = WO0 + 8
            for c in range(WO0 + 4 + AHEAD, head):
                low_part(c, c)
            with pool.Fori(0, 3) as n:
                for s in range(8):
                    low_part(8 * n + (head + s), head + s)
                    if s == 4:
                        pool.wait_ge(y_landed, 16 * 4)
                        for t in range(TOK):
                            pool.wait_ge(o_squared, 4 * n + (t + 2))
                            cols = bass.ds(SEQ * n, SEQ)
                            pool.tensor_tensor(y[:, t, cols], y[:, t, cols], fw[:, cols], ALU.mult).then_inc(o_gained, 1)

        @block.scalar
        def _(act):
            def high_part(c, s):
                act.wait_ge(w_landed[s % RAW], 8 * (c - s % RAW) + 16)
                if not isinstance(c, int) or c >= HL:
                    act.wait_ge(w_used, c - (HL - 1))
                act.activation(w_hi[:, s % HL, :], w_raw[:, s % RAW, :], ACT.Copy).then_inc(w_hi_ready, 1)

            def x_parts(j):
                act.wait_ge(x_landed[j % 2], 16 * (j // 2 + 1))
                for h in range(2):
                    k = 2 * j + h
                    ins = act.activation(x_hi[:, k, :], xs[:, j % 2, SEQ * h:SEQ * h + SEQ], ACT.Copy, scale=g_in[:, k:k + 1])
                ins.then_inc(x_hi_ready, 1)
                if j >= 3:
                    act.wait_ge(x_summed, j - 2)
                act.activation(acc[:, :] if j == 0 else sq[:, j % 2, :], xs[:, j % 2, :], ACT.Square).then_inc(x_squared, 1)

            act.dma_start(gain[:, :], gains[:, :]).then_inc(gains_landed, 16)
            act.dma_start(ident[:, :], tables[:, 0:P]).then_inc(tables_landed, 16)
            act.sem_inc(a_exp, 2)
            act.sem_inc(b_exp, 2)

            def preload(func):
                act.activation(preloaded[:, :], eps[:, :], func)

            act.wait_ge(consts_set, 1)
            preload(ACT.Copy)
            high_part(0, 0)
            act.wait_ge(gains_landed, 16)
            x_parts(0)
            high_part(1, 1)
            x_parts(1)
            high_part(2, 2)
            act.dma_start(cos_r[:, :], tables[:, P:P + SEQ]).then_inc(tables_landed, 16)
            act.dma_start(sin_r[:, :], tables[:, P + SEQ:P + 2 * SEQ]).then_inc(tables_landed, 16)

            def root(n, total, width):
                act.wait_ge(norm_total, n)
                act.wait_ge(consts_set, 1)
                act.activation(t2[:, :], total, ACT.Sqrt, bias=eps[:, :], scale=1.0 / width).then_inc(norm_root, 1)

            for c in range(GT0):
                if c + 2 < 8:
                    x_parts(c + 2)
                high_part(c + AHEAD, c + AHEAD)
                if c == CQ0:
                    root(1, B[7][:, :], D_MODEL)
                if c == QA0:
                    act.wait_ge(proj_evac, T_QA)
                    act.activation(sq[:, 0, :], ckv[:, :, :].rearrange("p a b -> p (a b)"), ACT.Square).then_inc(squares, 1)
                    act.activation(sq[:, 1, :], cq[:, 0:2, :].rearrange("p a b -> p (a b)"), ACT.Square).then_inc(squares, 1)
                    act.wait_ge(norm_sum, 1)
                    act.activation(acc[:, :], cq[:, 2:4, :].rearrange("p a b -> p (a b)"), ACT.Square).then_inc(squares, 1)
                if c == QA0 + 4:
                    root(2, B[4][:, :], KV_LORA)
                    act.wait_ge(norm_recip, 2)
                    root(3, B[5][:, :], Q_LORA)
                    act.wait_ge(lat_scaled, 1)
                    act.activation(ckv_hi[:, :, :], ckv[:, :, :], ACT.Copy).then_inc(lat_hi, 1)

            def a_split(t):
                act.wait_ge(a_pv, 4 * t + 1)
                g = t // 2
                act.activation(ks_hi[:, :], k_dup[:, bass.ds(g, 1), :].rearrange("p a b -> p (a b)"), ACT.Copy)
                act.activation(qs[0:64, :, 0, :], mixed[0:64, bass.ds(2 * t, 2), :], ACT.Copy).then_inc(a_split_hi, 1)
                act.activation(qs[64:128, :, 1, :], mixed[64:128, bass.ds(2 * t, 2), :], ACT.Copy).then_inc(a_split_hi, 1)
                act.activation(va_hi[:, :, 0, 0:64], v_f[:, :, bass.ds(64 * g, 64)], ACT.Copy)
                act.activation(va_hi[:, :, 1, 64:128], v_f[:, :, bass.ds(64 * g, 64)], ACT.Copy).then_inc(a_split_hi, 1)

            def a_exps(t, u):
                i, slot = u // 2, u % 2
                w = 2 * CHUNK if i == 0 else 3 * CHUNK
                act.wait_ge(a_turned, A_UNITS * t + u + 1)
                act.wait_ge(a_shift, A_UNITS * t + u + 1)
                st = st_a[:, slot, :, :]
                for e in range(2):
                    act.activation(pa[:, slot, e, 4 * CHUNK - w:], B[4 + slot][:, 192 * e + 192 - w:192 * e + 192], ACT.Exp,
                                   bias=st[:, 1, e:e + 1], scale=A_SCALE, accum_out=st[:, 3, e:e + 1])
                act.activation(st[:, 4, :], st[:, 2, :], ACT.Exp).then_inc(a_exp, 1)

            def a_pt_high(t, u):
                i, m = u // 2, u % 2
                act.wait_ge(a_turned, A_UNITS * t + u + 3)
                if m == 0:
                    act.wait_ge(a_pv, TOK * t + i + 1)
                ins = act.activation(pta_hi[:, m, 0:256], B[6][:, 0:256], ACT.Copy)
                if i > 0:
                    ins = act.activation(pta_hi[:, m, 256:384].rearrange("p (a b) -> p a b", a=2),
                                   B[6][:, 256:512].rearrange("p (a b) -> p a b", a=2)[:, :, 0:64], ACT.Copy)
                ins.then_inc(a_pt_hi, 1)

            act.wait_ge(a_zeroed, 1)
            act.wait_ge(v_kept, 1)
            act.wait_ge(rotated, 9)
            with act.Fori(0, 4) as t:
                for hf in range(16):
                    if hf == 0:
                        a_split(t)
                    if hf % 2 == 0:
                        high_part(8 * t + (GT0 + AHEAD + hf // 2), GT0 + AHEAD + hf // 2)
                    if hf in AT_TRANSPOSE:
                        a_pt_high(t, AT_TRANSPOSE[hf])
                    if hf in AT_SCORES:
                        a_exps(t, AT_SCORES[hf])
                for ct in range(4):
                    act.wait_ge(gate_evac, 4 * t + (TOK + ct + 1))
                    dst = gate_tmp[:, ct, :] if ct < 2 else mixed[:, bass.ds(2 * t + (A_TILES + ct - 2), 1), :].rearrange("p a b -> p (a b)")
                    act.activation(dst, dst, ACT.Silu).then_inc(gate_silu, 1)

            def b_rotary_high(p):
                par = p % 2
                act.wait_ge(b_rot, p + 1)
                act.activation(qr[par][0:64, 0, :], t3[0:64, :], ACT.Copy)
                act.activation(qr[par][64:128, 1, :], t3[64:128, :], ACT.Copy).then_inc(b_rot_hi, 1)

            def b_tile_high(p, j):
                idx, n = PB_TILES * p + j, 6 * p + SPLIT[j]
                par, bk = p % 2, B[idx % 4]
                scale = B_SCALE if j >= 5 else 1.0
                act.wait_ge(proj_done, T_PB + idx + 1)
                if p > 0:
                    act.wait_ge(b_lo, n - 1)
                    act.activation(b_tmp[:, n % 2, :], bk[:, :], ACT.Copy, scale=scale)
                if j in (1, 2):
                    dst, src = vb_hi[par][:, 2 * j - 2:2 * j, :], bk[:, :].rearrange("p (a b) -> p a b", a=2)
                else:
                    dst, src = {0: kn_hi, 3: kn_hi, 5: qn_hi, 6: qn_hi}[j][par][:, {0: 0, 3: 1, 5: 0, 6: 1}[j], :], bk[:, :]
                act.activation(dst, src, ACT.Copy, scale=scale).then_inc(b_hi, 1)

            def b_expo(w):
                u = w % 8
                n = P * (u % 4 + 1)
                act.wait_ge(b_turned, w + 1)
                act.wait_ge(b_max, w + 1)
                act.activation(pb[:, u % 4, 0:n], B[4 + u % 2][:, 0:n], ACT.Exp, bias=st_b[:, u % 4, 0:1],
                               accum_out=st_b[:, u % 4, 2:3]).then_inc(b_exp, 1)

            def b_pt_high(w):
                i = w % 4
                act.wait_ge(b_turned, w + 5)
                if i == 0:
                    act.wait_ge(b_pv, w // 4 + 1)
                act.activation(ptb_hi[:, 0:i + 1, P * i:P * i + P], B[6][:, 0:P * (i + 1)].rearrange("p (a b) -> p a b", a=i + 1),
                               ACT.Copy).then_inc(b_pt_hi, 1)

            def mixed_high(j):
                if j == 0:
                    act.wait_ge(lat_lo, 2 + CQ_T)
                elif j < 4 or j == 6:
                    act.wait_ge(b_pv, 7)
                elif j < 6:
                    act.wait_ge(proj_done, T_PB + PAIRS * PB_TILES)
                elif j == 7:
                    act.wait_ge(b_pv, 9)
                if j >= 4:
                    act.wait_ge(b_out, 2 * (j - 4) + 3)
                act.activation(mx_hi[j][:, :, :], mixed[:, 2 * j:2 * j + 2, :], ACT.Copy).then_inc(m_hi, 1)

            act.wait_ge(w_used, PB0)
            b_tile_high(0, 0)
            for k in range(CQ_T):
                act.activation(cqs_hi[:, k, :], cq[:, k, :], ACT.Copy).then_inc(cqs_split, 1)
            act.wait_ge(gated, 8)
            act.dma_start(cos_b[:, :], tables[:, P:P + SEQ]).then_inc(rot_landed, 16)
            act.dma_start(sin_b[:, :], tables[:, P + SEQ:P + 2 * SEQ]).then_inc(rot_landed, 16)
            for j in (1, 2, 3):
                b_tile_high(0, j)
            for c in range(PB0 + AHEAD, PB0 + AHEAD + 2):
                high_part(c, c)
            preload(ACT.Exp)
            b_tile_high(0, 5)
            b_rotary_high(0)
            b_tile_high(0, 6)
            high_part(PB0 + AHEAD + 2, PB0 + AHEAD + 2)
            for p in range(PAIRS):
                f = 0
                for step in B_STEPS:
                    w = 8 * p + (int(step[1]) if step[0] in "ST" else 0)
                    if step[0] == "S":
                        b_expo(w)
                    elif step[0] == "T":
                        b_pt_high(w)
                    elif step[0] == "F":
                        if p < PAIRS - 1:
                            if f == 8:
                                b_rotary_high(p + 1)
                            if f in B_SPLITS:
                                b_tile_high(p + 1, B_SPLITS[f])
                            if f in B_CHUNKS:
                                c = PB0 + 3 * (p + 1) + B_CHUNKS[f] + AHEAD
                                high_part(c, c)
                            if p == PAIRS - 2 and f == 6:
                                mixed_high(0)
                        else:
                            if f in M_AT:
                                mixed_high(M_AT[f])
                            done = sum(OUT_PIECES[:f])
                            for piece in range(done, done + OUT_PIECES[f]):
                                if piece % 4 == 0:
                                    c = WO0 + piece // 4 + AHEAD
                                    high_part(c, c)
                        f += 1

            act.wait_ge(b_pv, 9)
            for n in range(4):
                act.dma_start(y[:, :, SEQ * n:SEQ * n + SEQ], x_nat[0, :, SEQ * n:SEQ * n + SEQ].rearrange("(t p) d -> p t d", p=P))\
                    .then_inc(y0_landed if n == 0 else y_landed, 16)
            act.dma_start(fw[:, :], final_w[:, :]).then_inc(y_landed, 16)
            mixed_high(7)

            def out_squares(n):
                for t in range(TOK):
                    act.wait_ge(o_evac, 4 * n + (t + 5))
                    act.wait_ge(o_squared, 4 * n + (t + 1))
                    act.activation(junk[:, :], y[:, t, bass.ds(SEQ * n, SEQ)], ACT.Square, accum_out=sumsq[:, t, bass.ds(n, 1)]).then_inc(o_squared, 1)

            act.sem_inc(o_squared, 1)
            for s in range(4, 8):
                c = WO0 + AHEAD + s
                high_part(c, c)
            out_squares(0)
            with act.Fori(1, 3) as n:
                for s in range(8):
                    high_part(8 * n + (WO0 + AHEAD + s), WO0 + AHEAD + s)
                out_squares(n)
            for s in range(8 - AHEAD):
                c = WO0 + 24 + AHEAD + s
                high_part(c, c)
            for t in range(TOK):
                act.wait_ge(o_evac, 12 + t + 5)
                act.wait_ge(o_squared, 12 + t + 1)
                act.activation(junk[:, :], y[:, t, 3 * SEQ:], ACT.Square, accum_out=sumsq[:, t, 3:4]).then_inc(o_squared, 1)
                act.wait_ge(o_sum, t + 1)
                act.activation(fin[:, t, 1:2], fin[:, t, 0:1], ACT.Sqrt, bias=eps[:, :], scale=1.0 / D_MODEL).then_inc(o_root, 1)
                act.wait_ge(o_recip, t + 1)
                act.wait_ge(o_gained, 8 + t + 1 if t < 3 else 12)
                act.activation(y[:, t, 0:CE], y[:, t, 0:CE], ACT.Copy, scale=fin[:, t, 2:3]).then_inc(o_scaled_act, 1)

        @block.vector
        def _(dve):
            dve.memset(eps[:, :], EPS).then_inc(consts_set, 1)
            dve.memset(ones[:, :], 1.0).then_inc(consts_set, 1)
            dve.memset(mask_bf[:, :, :, :], 0.0).then_inc(consts_set, 1)
            dve.wait_ge(consts_set, 3)
            dve.memset(mask_bf[64:128, 0, :, :], MASK_VALUE)
            dve.memset(mask_bf[0:64, 1, :, :], MASK_VALUE).then_inc(consts_set, 1)
            dve.sem_inc(a_pt_lo, 1)
            dve.sem_inc(a_out, 1)
            dve.sem_inc(b_pt_lo, 1)
            dve.sem_inc(b_out, 1)
            dve.sem_inc(o_evac, 4)
            dve.wait_ge(gains_landed, 16)
            dve.tensor_scalar(neg_sinks[:, :], sinks, -1.0, None, ALU.mult).then_inc(consts_set, 1)
            dve.wait_ge(w_hi_ready, 1)
            dve.tensor_tensor(w_lo[:, 0, :], w_raw[:, 0, :], w_hi[:, 0, :].bitcast(F32), ALU.subtract).then_inc(w_lo_ready, 1)

            for j in range(8):
                dve.wait_ge(x_hi_ready, j + 1)
                for h in range(2):
                    k = 2 * j + h
                    ins = dve.scalar_tensor_tensor(out=x_lo[:, k, :], in0=xs[:, j % 2, SEQ * h:SEQ * h + SEQ], scalar=g_in[:, k:k + 1],
                                                   op0=ALU.mult, in1=x_hi[:, k, :].bitcast(F32), op1=ALU.subtract)
                ins.then_inc(x_lo_ready, 1)
                if j >= 1:
                    dve.wait_ge(x_squared, j + 1)
                    if j >= 2:
                        dve.wait_ge(x_summed, j - 1)
                    dve.tensor_tensor(acc[:, :], acc[:, :], sq[:, j % 2, :], ALU.add).then_inc(x_summed, 1)
            dve.wait_ge(tables_landed, 48)
            dve.tensor_copy(ident_bf[:, :], ident[:, :]).then_inc(consts_set, 1)
            dve.wait_ge(x_summed, 7)
            dve.tensor_tensor(t1[:, :], acc[:, 0:SEQ], acc[:, SEQ:CE], ALU.add).then_inc(norm_sum, 1)
            dve.wait_ge(norm_root, 1)
            dve.reciprocal(rstd[:, :], t2[:, :]).then_inc(norm_recip, 1)
            dve.wait_ge(norm_recip, 1)
            dve.tensor_tensor(cos_r[:, :], cos_r[:, :], rstd[:, :], ALU.mult)
            dve.tensor_tensor(sin_r[:, :], sin_r[:, :], rstd[:, :], ALU.mult).then_inc(consts_set, 1)
            dve.wait_ge(consts_set, 7)

            def rotate_terms(src, cos, sin, count, evac=proj_evac):
                dve.tensor_tensor(t1[:, :], src[:, :], cos[:, :], ALU.mult)
                for q in range(4):
                    o = q ^ 1
                    ins = dve.tensor_tensor(t2[32 * q:32 * q + 32, :], src[32 * o:32 * o + 32, :], sin[32 * q:32 * q + 32, :], ALU.mult)
                ins.then_inc(evac, 1)
                dve.wait_ge(evac, count)

            dve.wait_ge(proj_done, 1)
            rotate_terms(B[0], cos_r, sin_r, 1)
            for g in range(A_KV_HEADS):
                for h in range(2):
                    ins = dve.tensor_tensor(k_dup[64 * h:64 * h + 64, g, :], t1[64 * g:64 * g + 64, :], t2[64 * g:64 * g + 64, :], ALU.add)
            ins.then_inc(rotated, 1)
            dve.wait_ge(proj_done, 2)
            dve.tensor_tensor(v_t[:, :], B[1][:, :], rstd[:, :], ALU.mult).then_inc(proj_evac, 1)
            for j in range(CKV_T):
                dve.wait_ge(proj_done, 3 + j)
                dve.tensor_tensor(ckv[:, j, :], B[2 + j][:, :], rstd[:, :], ALU.mult).then_inc(proj_evac, 1)
            for j in range(CQ_T):
                dve.wait_ge(proj_done, T_CQ + 1 + j)
                dve.tensor_tensor(cq[:, j, :], B[4 + j][:, :], rstd[:, :], ALU.mult).then_inc(proj_evac, 1)
            dve.wait_ge(squares, 3)
            dve.tensor_tensor(t3[:, :], sq[:, 0, 0:SEQ], sq[:, 0, SEQ:CE], ALU.add).then_inc(norm_sum, 1)
            dve.tensor_tensor(sq[:, 1, :], sq[:, 1, :], acc[:, :], ALU.add).then_inc(squares, 1)
            dve.wait_ge(squares, 4)
            dve.wait_ge(norm_sum, 2)
            dve.tensor_tensor(sq[:, 0, 0:SEQ], sq[:, 1, 0:SEQ], sq[:, 1, SEQ:CE], ALU.add).then_inc(norm_sum, 1)
            dve.wait_ge(norm_root, 2)
            dve.reciprocal(t3[:, :], t2[:, :]).then_inc(norm_recip, 1)
            dve.wait_ge(norm_recip, 2)
            for j in range(CKV_T):
                ins = dve.scalar_tensor_tensor(out=ckv[:, j, :], in0=ckv[:, j, :], scalar=g_kv[:, j:j + 1], op0=ALU.mult,
                                               in1=t3[:, :], op1=ALU.mult)
            ins.then_inc(lat_scaled, 1)
            dve.wait_ge(norm_root, 3)
            dve.wait_ge(lat_scaled, 1)
            dve.reciprocal(t3[:, :], t2[:, :]).then_inc(norm_recip, 1)
            dve.wait_ge(norm_recip, 3)
            for j in range(CQ_T):
                ins = dve.scalar_tensor_tensor(out=cq[:, j, :], in0=cq[:, j, :], scalar=g_q[:, j:j + 1], op0=ALU.mult,
                                               in1=t3[:, :], op1=ALU.mult)
            ins.then_inc(lat_scaled, 1)
            dve.wait_ge(lat_hi, 1)
            dve.tensor_tensor(ckv_lo[:, :, :], ckv[:, :, :], ckv_hi[:, :, :].bitcast(F32), ALU.subtract).then_inc(lat_lo, 1)
            dve.wait_ge(v_turned, 1)
            dve.tensor_copy(v_f[:, :, :], B[6][:, :].rearrange("p (a b) -> p a b", a=TOK)).then_inc(v_kept, 1)
            dve.wait_ge(norm_total, 3)
            dve.wait_ge(lat_lo, 1)
            dve.memset(va_hi[:, :, 0, 64:128].bitcast(F32), 0.0)
            dve.memset(va_hi[:, :, 1, 0:64].bitcast(F32), 0.0)
            dve.memset(va_lo[:, :, 0, 64:128].bitcast(F32), 0.0)
            dve.memset(va_lo[:, :, 1, 0:64].bitcast(F32), 0.0)
            dve.memset(pa[:, :, :, :], 0.0).then_inc(a_zeroed, 1)
            dve.sem_inc(gate_evac, 3)
            for m in range(A_TILES):
                dve.wait_ge(proj_done, T_QA + 1 + m)
                dve.wait_ge(rotated, 1 + m)
                rotate_terms(B[m], cos_r, sin_r, T_QA + 1 + m)
                dve.tensor_tensor(mixed[:, m, :], t1[:, :], t2[:, :], ALU.add).then_inc(rotated, 1)
            dve.wait_ge(proj_done, T_KR + 1)
            dve.wait_ge(rotated, 1 + A_TILES)
            rotate_terms(B[3], cos_r, sin_r, 4, gate_evac)
            dve.wait_ge(lat_scaled, 2)
            dve.tensor_tensor(t3[:, :], t1[:, :], t2[:, :], ALU.add).then_inc(rotated, 1)

            def a_maxima(t, u):
                i, m, slot = u // 2, u % 2, u % 2
                w = 2 * CHUNK if i == 0 else 3 * CHUNK
                st = st_a[:, slot, :, :]
                hd = bass.ds(4 * t + 2 * m, 2)
                dve.wait_ge(a_scores, A_UNITS * t + u + 1)
                dve.reduce_max(st[:, 0, :], B[4 + slot][:, 0:384].rearrange("p (a b) -> p a b", a=2)[:, :, 192 - w:192], AX.X).then_inc(a_max, 1)
                dve.wait_ge(a_max, 2 * (A_UNITS * t + u) + 1)
                dve.scalar_tensor_tensor(out=st[:, 1, :], in0=st[:, 0, :], scalar=-A_SCALE, op0=ALU.mult,
                                         in1=neg_sinks[:, hd], op1=ALU.min).then_inc(a_max, 1)
                dve.wait_ge(a_max, 2 * (A_UNITS * t + u) + 2)
                dve.tensor_tensor(st[:, 2, :], st[:, 1, :], sinks[:, hd], ALU.add).then_inc(a_shift, 1)

            def a_normalise(t, u):
                slot = u % 2
                st = st_a[:, slot, :, :]
                dve.wait_ge(a_exp, A_UNITS * t + u + 3)
                dve.tensor_tensor(st[:, 5, :], st[:, 3, :], st[:, 4, :], ALU.add).then_inc(a_recip, 1)
                dve.wait_ge(a_recip, 2 * (A_UNITS * t + u) + 1)
                dve.reciprocal(st[:, 5, :], st[:, 5, :]).then_inc(a_recip, 1)
                dve.wait_ge(a_recip, 2 * (A_UNITS * t + u) + 2)
                for e in range(2):
                    ins = dve.tensor_scalar(pa[:, slot, e, CHUNK:], pa[:, slot, e, CHUNK:], st[:, 5, e:e + 1], None, ALU.mult)
                ins.then_inc(a_probs, 1)

            def a_pt_low(t, u):
                i, m = u // 2, u % 2
                dve.wait_ge(a_pt_hi, A_UNITS * t + u + 1)
                ins = dve.tensor_tensor(pta_lo[:, m, 0:256], B[6][:, 0:256], pta_hi[:, m, 0:256].bitcast(F32), ALU.subtract)
                if i > 0:
                    ins = dve.tensor_tensor(pta_lo[:, m, 256:384].rearrange("p (a b) -> p a b", a=2),
                                            B[6][:, 256:512].rearrange("p (a b) -> p a b", a=2)[:, :, 0:64],
                                            pta_hi[:, m, 256:384].bitcast(F32).rearrange("p (a b) -> p a b", a=2), ALU.subtract)
                ins.then_inc(a_pt_lo, 1)

            dve.wait_ge(rotated, 10)
            dve.tensor_copy(kr_hi[:, :], t3[:, :]).then_inc(lat_hi, 1)
            dve.wait_ge(lat_hi, 2)
            dve.tensor_tensor(kr_lo[:, :], t3[:, :], kr_hi[:, :].bitcast(F32), ALU.subtract).then_inc(lat_lo, 1)
            with dve.Fori(0, 4) as t:
                dve.wait_ge(a_split_hi, 3 * t + 1)
                g = t // 2
                dve.tensor_tensor(ks_lo[:, :], k_dup[:, bass.ds(g, 1), :].rearrange("p a b -> p (a b)"), ks_hi[:, :].bitcast(F32), ALU.subtract)
                dve.tensor_tensor(qs[64:128, :, 0, :], mixed[0:64, bass.ds(2 * t, 2), :], qs[0:64, :, 0, :].bitcast(F32), ALU.subtract)
                dve.wait_ge(a_split_hi, 3 * t + 2)
                dve.tensor_tensor(qs[0:64, :, 1, :], mixed[64:128, bass.ds(2 * t, 2), :], qs[64:128, :, 1, :].bitcast(F32), ALU.subtract)\
                    .then_inc(a_split_lo, 1)
                dve.wait_ge(a_split_hi, 3 * t + 3)
                for e in range(2):
                    ins = dve.tensor_tensor(va_lo[:, :, e, 64 * e:64 * e + 64], v_f[:, :, bass.ds(64 * g, 64)],
                                            va_hi[:, :, e, 64 * e:64 * e + 64].bitcast(F32), ALU.subtract)
                ins.then_inc(a_split_lo, 1)
                last = None
                for hf in range(17):
                    if last is not None:
                        a_normalise(t, last)
                        last = None
                    if hf in AT_SCORES:
                        a_maxima(t, AT_SCORES[hf])
                        last = AT_SCORES[hf]
                    if hf in AT_TRANSPOSE:
                        a_pt_low(t, AT_TRANSPOSE[hf])
                    if hf == 16:
                        for ct in range(4):
                            dve.wait_ge(proj_done, 4 * t + (T_GT + ct + 1))
                            dst = gate_tmp[:, ct, :] if ct < 2 else mixed[:, bass.ds(2 * t + (A_TILES + ct - 2), 1), :].rearrange("p a b -> p (a b)")
                            dve.tensor_tensor(dst, B[ct][:, :], rstd[:, :], ALU.mult).then_inc(gate_evac, 1)
                    if hf in AT_PV:
                        i = AT_PV[hf]
                        dve.wait_ge(a_pv, TOK * t + i + 2)
                        dve.tensor_scalar(mixed[:, bass.ds(2 * t, 2), P * i:P * i + P], B[7][:, 0:256].rearrange("p (a b) -> p a b", a=2),
                                          1.0, None, ALU.mult).then_inc(a_out, 1)
                dve.wait_ge(a_out, TOK * t + 5)
                for ct in range(2):
                    dve.wait_ge(gate_silu, 4 * t + (ct + 1))
                    m = mixed[:, bass.ds(2 * t + ct, 1), :].rearrange("p a b -> p (a b)")
                    dve.tensor_tensor(m, m, gate_tmp[:, ct, :], ALU.mult).then_inc(gated, 1)
                dve.wait_ge(gated, 2 * t + 2)

            def b_rotary(p, part):
                if part == 0:
                    bk = B[(PB_TILES * p + 4) % 4]
                    dve.wait_ge(proj_done, T_PB + PB_TILES * p + 5)
                    if p > 0:
                        dve.wait_ge(b_rot_lo, p)
                    dve.tensor_tensor(t1[:, :], bk[:, :], cos_b[:, :], ALU.mult)
                    for q in range(4):
                        o = q ^ 1
                        ins = dve.tensor_tensor(t2[32 * q:32 * q + 32, :], bk[32 * o:32 * o + 32, :], sin_b[32 * q:32 * q + 32, :], ALU.mult)
                    ins.then_inc(b_rot_evac, 1)
                else:
                    dve.wait_ge(b_rot_evac, p + 1)
                    dve.tensor_tensor(t3[:, :], t1[:, :], t2[:, :], ALU.add).then_inc(b_rot, 1)

            def b_tile_low(j):
                par, bk = 0, B[j % 4]
                dve.wait_ge(b_hi, SPLIT[j] + 1)
                if j >= 5:
                    hi, lo = qn_hi[0][:, j - 5, :], qn_lo[0][:, j - 5, :]
                    dve.scalar_tensor_tensor(out=lo, in0=bk[:, :], scalar=B_SCALE, op0=ALU.mult, in1=hi.bitcast(F32), op1=ALU.subtract)\
                        .then_inc(b_lo, 1)
                    return
                if j in (1, 2):
                    dst, hi, src = vb_lo[par][:, 2 * j - 2:2 * j, :], vb_hi[par][:, 2 * j - 2:2 * j, :], bk[:, :].rearrange("p (a b) -> p a b", a=2)
                else:
                    dst, hi, src = kn_lo[par][:, j // 3, :], kn_hi[par][:, j // 3, :], bk[:, :]
                dve.tensor_tensor(dst, src, hi.bitcast(F32), ALU.subtract).then_inc(b_lo, 1)

            def b_rotary_low(p):
                par = p % 2
                dve.wait_ge(b_rot_hi, p + 1)
                dve.tensor_tensor(qr[par][64:128, 0, :], t3[0:64, :], qr[par][0:64, 0, :].bitcast(F32), ALU.subtract)
                dve.tensor_tensor(qr[par][0:64, 1, :], t3[64:128, :], qr[par][64:128, 1, :].bitcast(F32), ALU.subtract).then_inc(b_rot_lo, 1)

            def b_maxima(w):
                u = w % 8
                n = P * (u % 4 + 1)
                dve.wait_ge(b_scores, w + 1)
                dve.reduce_max(st_b[:, u % 4, 0:1], B[4 + u % 2][:, 0:n], AX.X, negate=True).then_inc(b_max, 1)

            def b_normalise(w):
                u = w % 8
                n = P * (u % 4 + 1)
                dve.wait_ge(b_exp, w + 3)
                dve.reciprocal(st_b[:, u % 4, 3:4], st_b[:, u % 4, 2:3]).then_inc(b_recip, 1)
                dve.wait_ge(b_recip, w + 1)
                dve.tensor_scalar(pb[:, u % 4, 0:n], pb[:, u % 4, 0:n], st_b[:, u % 4, 3:4], None, ALU.mult).then_inc(b_probs, 1)

            def b_pt_low(w):
                i = w % 4
                dve.wait_ge(b_pt_hi, w + 1)
                dve.tensor_tensor(ptb_lo[:, 0:i + 1, P * i:P * i + P], B[6][:, 0:P * (i + 1)].rearrange("p (a b) -> p a b", a=i + 1),
                                  ptb_hi[:, 0:i + 1, P * i:P * i + P].bitcast(F32), ALU.subtract).then_inc(b_pt_lo, 1)

            def b_take(head):
                dve.wait_ge(b_pv, head + 2)
                m = mixed[:, A_TILES + head, :]
                dve.tensor_tensor(m, B[7][:, :], m, ALU.mult).then_inc(b_out, 1)

            b_tile_low(0)
            for k in range(CQ_T):
                dve.wait_ge(cqs_split, k + 1)
                dve.tensor_tensor(cqs_lo[:, k, :], cq[:, k, :], cqs_hi[:, k, :].bitcast(F32), ALU.subtract).then_inc(lat_lo, 1)
            for j in (1, 2, 3):
                b_tile_low(j)
            dve.wait_ge(rot_landed, 32)
            dve.tensor_scalar(cos_b[:, :], cos_b[:, :], B_SCALE, None, ALU.mult)
            dve.tensor_scalar(sin_b[:, :], sin_b[:, :], B_SCALE, None, ALU.mult).then_inc(consts_set, 1)
            dve.wait_ge(consts_set, 8)
            for part in range(2):
                b_rotary(0, part)
            b_tile_low(5)
            b_rotary_low(0)
            b_tile_low(6)
            dve.wait_ge(gate_silu, 16)
            for p in range(PAIRS):
                f, late = 0, None
                for step in B_STEPS:
                    w = 8 * p + (int(step[1]) if step[0] in "ST" else 0)
                    if step[0] == "S":
                        if late is not None:
                            b_normalise(late)
                        b_maxima(w)
                        late = w
                        continue
                    if step[0] == "T":
                        if late is not None:
                            b_normalise(late)
                            late = None
                        b_pt_low(w)
                    elif step == "V0":
                        continue
                    elif step == "L":
                        if p > 0:
                            b_take(2 * p - 1)
                        continue
                    else:
                        if p < PAIRS - 1:
                            if f in B_ROTARY:
                                b_rotary(p + 1, B_ROTARY[f])
                            if f == 8:
                                b_rotary_low(p + 1)
                        if f == 9:
                            b_take(2 * p)
                        f += 1
                    if late is not None:
                        b_normalise(late)
                        late = None

            b_take(B_HEADS - 1)

            dve.wait_ge(m_hi, 8)
            dve.tensor_tensor(mx_lo[7][:, :, :], mixed[:, 14:16, :], mx_hi[7][:, :, :].bitcast(F32), ALU.subtract).then_inc(m_lo, 1)
            dve.wait_ge(y0_landed, 16)

            def residual(n, t):
                dve.wait_ge(o_done, 4 * n + (t + 1))
                ys = y[:, t, bass.ds(SEQ * n, SEQ)]
                dve.tensor_tensor(ys, B[t][:, :], ys, ALU.add).then_inc(o_evac, 1)

            for t in range(TOK):
                residual(0, t)
            dve.wait_ge(y_landed, 64)
            with dve.Fori(1, 3) as n:
                for t in range(TOK):
                    residual(n, t)
            for t in range(TOK):
                residual(3, t)
                dve.wait_ge(o_squared, 12 + t + 2)
                dve.reduce_sum(fin[:, t, 0:1], sumsq[:, t, :], AX.X).then_inc(o_sum, 1)
                dve.wait_ge(o_root, t + 1)
                dve.reciprocal(fin[:, t, 2:3], fin[:, t, 1:2]).then_inc(o_recip, 1)
                dve.wait_ge(o_recip, t + 1)
                ys = y[:, t, 3 * SEQ:]
                dve.scalar_tensor_tensor(out=ys, in0=ys, scalar=fin[:, t, 2:3], op0=ALU.mult, in1=fw[:, 3 * SEQ:], op1=ALU.mult)
                dve.wait_ge(o_gained, 12)
                ys = y[:, t, 2 * SEQ:3 * SEQ]
                dve.tensor_scalar(ys, ys, fin[:, t, 2:3], None, ALU.mult).then_inc(o_scaled, 1)

        @block.tensor
        def _(pe):
            def three(dst, ah, al, bh, bl, start, stop, frees_chunk=False):
                ins = pe.matmul(dst, ah, bh, start=start, stop=False)
                if frees_chunk:
                    ins.then_inc(w_used, 1)
                pe.matmul(dst, al, bh, start=False, stop=False)
                return pe.matmul(dst, ah, bl, start=False, stop=stop)

            def columns(s, banks, tiles, ks, frees_chunk, width=SEQ):
                for ct in tiles:
                    for n, k in enumerate(ks):
                        o = width * n + P * ct
                        ins = three(B[banks[ct]][:, :], w_hi[:, s % HL, o:o + P], w_lo[:, s % HL, o:o + P],
                                    x_hi[:, k, :], x_lo[:, k, :], k == 0, k == K_IN - 1, frees_chunk and ct == tiles[0] and n == 0)
                    if ks[-1] == K_IN - 1:
                        ins.then_inc(proj_done, 1)

            pe.sem_inc(a_turned, 2)
            pe.sem_inc(a_pv, 1)
            pe.sem_inc(b_turned, 4)
            pe.sem_inc(b_pv, 1)
            pe.wait_ge(w_hi_ready, 1)
            pe.wait_ge(x_hi_ready, 1)
            for ct in range(4):
                for k in range(2):
                    o = SEQ * k + P * ct
                    pe.matmul(B[ct][:, :], w_hi[:, 0, o:o + P], x_hi[:, k, :], start=k == 0, stop=False)
            pe.wait_ge(w_lo_ready, 1)
            pe.wait_ge(x_lo_ready, 1)
            for ct in range(4):
                for k in range(2):
                    o = SEQ * k + P * ct
                    pe.matmul(B[ct][:, :], w_lo[:, 0, o:o + P], x_hi[:, k, :], start=False, stop=False)
                    pe.matmul(B[ct][:, :], w_hi[:, 0, o:o + P], x_lo[:, k, :], start=False, stop=False)
            for s in range(1, 8):
                pe.wait_ge(w_lo_ready, KV0 + s + 1)
                pe.wait_ge(x_lo_ready, s + 1)
                for ct in range(4):
                    columns(KV0 + s, (0, 1, 2, 3), (ct,), (2 * s, 2 * s + 1), ct == 0)
            pe.wait_ge(consts_set, 2)
            pe.wait_ge(norm_sum, 1)
            pe.matmul(B[7][:, :], ones[:, :], t1[:, :], start=True, stop=True).then_inc(norm_total, 1)
            for s in range(8):
                pe.wait_ge(w_lo_ready, CQ0 + s + 1)
                for ct in range(4):
                    if s == 0 and ct == 3:
                        pe.wait_ge(norm_root, 1)
                    columns(CQ0 + s, (4, 5, 6, 7), (ct,), (2 * s, 2 * s + 1), ct == 0)
            for s in range(16):
                first = s < 8
                pe.wait_ge(w_lo_ready, QA0 + s + 1)
                for ct in range(4):
                    if s == 0:
                        pe.wait_ge(proj_evac, ct + 1)
                    if s == 8 and ct == 0:
                        pe.wait_ge(norm_root, 3)
                        pe.wait_ge(v_kept, 1)
                    columns(QA0 + s, (0, 1, 2, 3) if first else (4, 5, 6, 7), (ct,), (2 * (s % 8), 2 * (s % 8) + 1), ct == 0)
                if s == 3:
                    pe.wait_ge(proj_evac, T_QA)
                    pe.wait_ge(tables_landed, 48)
                    for t in range(TOK):
                        ins = pe.transpose(B[6][:, P * t:P * t + P], v_t[:, P * t:P * t + P], ident[:, :])
                    ins.then_inc(v_turned, 1)
                    pe.wait_ge(norm_sum, 2)
                    pe.matmul(B[4][:, :], ones[:, :], t3[:, :], start=True, stop=True).then_inc(norm_total, 1)
                    pe.wait_ge(norm_sum, 3)
                    pe.matmul(B[5][:, :], ones[:, :], sq[:, 0, 0:SEQ], start=True, stop=True).then_inc(norm_total, 1)
            pe.wait_ge(proj_evac, T_QA + 4)
            for s in range(2):
                pe.wait_ge(w_lo_ready, KR0 + s + 1)
                columns(KR0 + s, (3,), (0,), tuple(range(8 * s, 8 * s + 8)), True, width=P)

            def a_score(t, u):
                i, m, slot = u // 2, u % 2, u % 2
                w = 2 * CHUNK if i == 0 else 3 * CHUNK
                pe.wait_ge(a_exp, A_UNITS * t + u + 1)
                k0 = P * (i + 1) - w
                for e in range(2):
                    dst = B[4 + slot][:, 192 * e + 192 - w:192 * e + 192]
                    q = qs[:, m, e, P * i:P * i + P]
                    pe.matmul(dst, q, ks_hi[:, k0:k0 + w], start=e == 0, stop=False)
                    pe.matmul(dst, q, ks_lo[:, k0:k0 + w], start=False, stop=False)
                both = B[4 + slot][:, 0:384].rearrange("p (a b) -> p a b", a=2)
                if i > 0:
                    pe.matmul(both[:, :, 0:CHUNK], ident_bf[:, :], mask_bf[:, 0, :, :], start=False, stop=False)
                pe.matmul(both[:, :, 2 * CHUNK:3 * CHUNK], ident_bf[:, :], mask_bf[:, 1, :, :], start=False, stop=True).then_inc(a_scores, 1)

            def a_transpose(t, u):
                i, slot = u // 2, u % 2
                pe.wait_ge(a_probs, A_UNITS * t + u + 1)
                pe.wait_ge(a_pt_lo, A_UNITS * t + u + 1)
                for e in range(2):
                    ins = pe.transpose(B[6][:, P * e:P * e + P], pa[:, slot, e, 2 * CHUNK:], ident[:, :])
                if i > 0:
                    for e in range(2):
                        ins = pe.transpose(B[6][:, 256 + P * e:256 + P * e + P], pa[:, slot, e, 0:2 * CHUNK], ident[:, :])
                ins.then_inc(a_turned, 1)

            def a_product(t, i):
                pe.wait_ge(a_pt_lo, A_UNITS * t + 2 * i + 3)
                pe.wait_ge(a_out, TOK * t + i + 1)
                if i == 0:
                    pe.wait_ge(a_split_lo, 2 * t + 2)
                dst = B[7][:, 0:256].rearrange("p (a b) -> p a b", a=2)
                for e in range(2):
                    ins = three(dst, va_hi[:, i, e, :], va_lo[:, i, e, :], pta_hi[:, :, P * e:P * e + P], pta_lo[:, :, P * e:P * e + P],
                                e == 0, i == 0 and e == 1)
                if i > 0:
                    for e in range(2):
                        o = 256 + CHUNK * e
                        ins = three(dst[:, :, 0:CHUNK], va_hi[:, i - 1, e, :], va_lo[:, i - 1, e, :],
                                    pta_hi[:, :, o:o + CHUNK], pta_lo[:, :, o:o + CHUNK], False, e == 1)
                ins.then_inc(a_pv, 1)

            pe.wait_ge(consts_set, 6)
            with pe.Fori(0, 4) as t:
                for hf in range(16):
                    if hf in AT_PV:
                        a_product(t, AT_PV[hf])
                    if hf in AT_TRANSPOSE:
                        a_transpose(t, AT_TRANSPOSE[hf])
                    if hf in AT_SCORES:
                        if AT_SCORES[hf] == 0:
                            pe.wait_ge(proj_evac, T_KR)
                            pe.wait_ge(a_split_lo, 2 * t + 1)
                        a_score(t, AT_SCORES[hf])
                    s = hf // 2
                    if hf % 2 == 0:
                        pe.wait_ge(w_lo_ready, 8 * t + (GT0 + s + 1))
                    for ct in (0, 1) if hf % 2 == 0 else (2, 3):
                        if s == 0:
                            pe.wait_ge(gate_evac, 4 * t + (ct + 1))
                        columns(GT0 + s, (0, 1, 2, 3), (ct,), (2 * s, 2 * s + 1), ct == 0)
                a_product(t, AT_PV[16])

            def bank_free(idx):
                if idx < 4:
                    pe.wait_ge(gate_evac, 4 * 4 + idx + 1)
                    return
                p, j = divmod(idx - 4, PB_TILES)
                if j == 4:
                    pe.wait_ge(b_rot_evac, p + 1)
                elif p == 0:
                    pe.wait_ge(b_lo, SPLIT[j] + 1)
                else:
                    pe.wait_ge(b_hi, 6 * p + SPLIT[j] + 1)

            def b_project(p, j, ks):
                idx = PB_TILES * p + j
                bk = B[idx % 4]
                c = PB0 + 3 * p + CHUNK_OF_TILE[j]
                slot = c % HL
                last = ks[-1] == (CKV_T if j < 4 else CQ_T) - 1
                if ks[0] == 0:
                    bank_free(idx)
                    pe.wait_ge(w_lo_ready, c + 1)
                if j in (1, 2):
                    for tt in range(2):
                        tok = 2 * (j - 1) + tt
                        for k in ks:
                            o = 512 + 256 * k
                            ins = three(bk[:, 256 * tt:256 * tt + 256], ckv_hi[:, k, P * tok:P * tok + P], ckv_lo[:, k, P * tok:P * tok + P],
                                        w_hi[:, slot, o:o + 256], w_lo[:, slot, o:o + 256], k == 0, k == CKV_T - 1)
                else:
                    rhs_hi, rhs_lo = (ckv_hi, ckv_lo) if j < 4 else (cqs_hi, cqs_lo)
                    step = P if j == 4 else 2 * P
                    for k in ks:
                        o = step * k + (P if j in (3, 6) else 0)
                        if p == 0 and j == 4:
                            pe.wait_ge(lat_lo, 3 + k)
                        ins = three(bk[:, :], w_hi[:, slot, o:o + P], w_lo[:, slot, o:o + P], rhs_hi[:, k, :], rhs_lo[:, k, :],
                                    k == 0, last and k == ks[-1], k == 0 and j in (0, 4, 5))
                if last:
                    ins.then_inc(proj_done, 1)

            def b_score(w):
                h, i, par = w % 8 // 4, w % 4, w // 8 % 2
                n = P * (i + 1)
                pe.wait_ge(b_exp, w + 1)
                if i == 0:
                    pe.wait_ge(b_rot_lo, w // 8 + 1)
                    pe.wait_ge(b_lo, 6 * (w // 8) + 5 + h)
                dst = B[4 + w % 2][:, 0:n]
                q = slice(P * i, P * i + P)
                pe.matmul(dst, qr[par][:, h, q], kr_hi[:, 0:n], start=True, stop=False)
                pe.matmul(dst, qr[par][:, h, q], kr_lo[:, 0:n], start=False, stop=False)
                three(dst, qn_hi[par][:, h, q], qn_lo[par][:, h, q], kn_hi[par][:, h, 0:n], kn_lo[par][:, h, 0:n], False, False)
                pe.matmul(B[4 + w % 2][:, n - CHUNK:n], ident_bf[:, :], mask_bf[:, 1, 0, :], start=False, stop=True).then_inc(b_scores, 1)

            def b_transpose(w):
                pe.wait_ge(b_probs, w + 1)
                pe.wait_ge(b_pt_lo, w + 1)
                for kt in range(w % 4 + 1):
                    ins = pe.transpose(B[6][:, P * kt:P * kt + P], pb[:, w % 4, P * kt:P * kt + P], ident[:, :])
                ins.then_inc(b_turned, 1)

            def b_product(head):
                h, par = head % 2, head // 2 % 2
                pe.wait_ge(b_pt_lo, 4 * head + 5)
                pe.wait_ge(b_out, head + 1)
                if head == 0:
                    pe.wait_ge(a_out, 17)
                for kt in range(TOK):
                    v = slice(P * h, P * h + P)
                    ins = three(B[7][:, P * kt:SEQ], vb_hi[par][:, kt, v], vb_lo[par][:, kt, v],
                                ptb_hi[:, kt, P * kt:SEQ], ptb_lo[:, kt, P * kt:SEQ], kt == 0, kt == TOK - 1)
                ins.then_inc(b_pv, 1)

            def mixed_split(s):
                if s < 7:
                    pe.wait_ge(m_lo_pool, s + 1)
                else:
                    pe.wait_ge(m_lo, 1)

            def out_rows(n, s, t, frees_chunk):
                slot = (WO0 + s) % HL
                for kk in range(2):
                    ins = three(B[t][:, :], mx_hi[s][:, kk, P * t:P * t + P], mx_lo[s][:, kk, P * t:P * t + P],
                                w_hi[:, slot, SEQ * kk:SEQ * kk + SEQ], w_lo[:, slot, SEQ * kk:SEQ * kk + SEQ],
                                s == 0 and kk == 0, s == 7 and kk == 1, frees_chunk and kk == 0)
                if s == 7:
                    ins.then_inc(o_done, 1)

            for j in range(PB_TILES):
                b_project(0, j, (0, 1) if j < 4 else (0, 1, 2, 3))
            for p in range(PAIRS):
                f = 0
                for step in B_STEPS:
                    if step[0] == "S":
                        b_score(8 * p + int(step[1]))
                    elif step[0] == "T":
                        b_transpose(8 * p + int(step[1]))
                    elif step == "V0":
                        b_product(2 * p)
                    elif step == "L":
                        if p > 0:
                            b_product(2 * p - 1)
                    else:
                        if p < PAIRS - 1:
                            if p == 0 and f == 0:
                                pe.wait_ge(b_lo, 6)
                            for j, ks in B_PIECES[f]:
                                b_project(p + 1, j, ks)
                        else:
                            done = sum(OUT_PIECES[:f])
                            for piece in range(done, done + OUT_PIECES[f]):
                                s, t = divmod(piece, 4)
                                if t == 0:
                                    pe.wait_ge(w_lo_ready, WO0 + s + 1)
                                    mixed_split(s)
                                if s == 0:
                                    bank_free(PB_TILES * PAIRS + t)
                                out_rows(0, s, t, t == 0)
                        f += 1

            b_product(B_HEADS - 1)

            def out_chunks(n, chunks):
                for s in chunks:
                    pe.wait_ge(w_lo_ready, 8 * n + (WO0 + s + 1))
                    mixed_split(s)
                    for t in range(TOK):
                        if s == 0:
                            pe.wait_ge(o_evac, 4 * n + (t + 1))
                        out_rows(n, s, t, t == 0)

            out_chunks(0, range(4, 8))
            with pe.Fori(1, 3) as n:
                out_chunks(n, range(8))
            out_chunks(3, range(4))
            for t in range(TOK):
                for s in range(4, 8):
                    if t == 0:
                        pe.wait_ge(w_lo_ready, WO0 + 24 + s + 1)
                    out_rows(3, s, t, t == 0 and s == 4)


def laid_out_weights(w_in, w_q_b, w_kv_b, w_out):
    def cols(*parts):
        return np.concatenate(parts, axis=1)

    def chunked(w, ks):
        k, c = w.shape
        return w.reshape(k // (P * ks), ks, P, c).transpose(0, 2, 1, 3).reshape(-1, P, ks * c)

    a_w, kv_w = A_HEADS * A_DIM, A_KV_HEADS * A_DIM
    o = np.cumsum([0, a_w, kv_w, kv_w, a_w, Q_LORA, KV_LORA, B_ROPE, B_HEADS * B_V])
    a_q, a_k, a_v, a_g, b_cq, b_ckv, b_kr, b_g = (w_in[:, o[i]:o[i + 1]] for i in range(8))
    stream = [chunked(cols(a_k, a_v, b_ckv), 2), chunked(b_cq, 2), chunked(a_q[:, 0:SEQ], 2), chunked(a_q[:, SEQ:], 2),
              chunked(cols(b_kr, b_kr), 8)]
    for t in range(4):
        c = slice(2 * P * t, 2 * P * t + 2 * P)
        stream.append(chunked(cols(a_g[:, c], b_g[:, c]), 2))
    q = w_q_b.reshape(Q_LORA, B_HEADS, B_NOPE + B_ROPE)
    kv = w_kv_b.reshape(KV_LORA, B_HEADS, B_NOPE + B_V)
    pad = np.zeros((1, P, CE // 2), w_q_b.dtype)
    for p in range(B_HEADS // 2):
        h = slice(2 * p, 2 * p + 2)
        kn = chunked(kv[:, h, :B_NOPE].reshape(KV_LORA, -1), 2)
        v = chunked(kv[:, h, B_NOPE:].reshape(KV_LORA, -1), 2)
        qn = chunked(q[:, h, :B_NOPE].reshape(Q_LORA, -1), 4)
        qr = chunked(q[:, h, B_NOPE:].reshape(Q_LORA, -1), 4)
        stream += [np.concatenate([kn, v], axis=2), np.concatenate([qr, pad], axis=2), qn]
    for n in range(4):
        stream.append(chunked(w_out[:, SEQ * n:SEQ * n + SEQ], 2))
    stream = np.concatenate(stream, axis=0)
    assert stream.shape == (CHUNKS, P, CE)
    return np.ascontiguousarray(stream)


def rotary_tables():
    half = A_DIM // 2
    inv_freq = np.float32(1) / (np.float32(10000.0) ** (np.arange(0, A_DIM, 2, dtype=np.float32) / np.float32(A_DIM)))
    ang = np.arange(SEQ, dtype=np.float32)[None, :] * inv_freq.astype(np.float32)[:, None]
    cos, sin = np.cos(ang.astype(np.float64)), np.sin(ang.astype(np.float64))
    assert half == 32 and A_DIM == B_ROPE
    cos = np.concatenate([cos] * 4, axis=0)
    sin = np.concatenate([-sin, sin] * 2, axis=0)
    return np.ascontiguousarray(np.concatenate([np.eye(P), cos, sin], axis=1).astype(np.float32))


def kernel(x, norm_in_w, w_in, sinks_a, q_a_norm_w, w_q_b, kv_a_norm_w, w_kv_b, w_out, final_norm_w):
    import concourse.bacc as bacc
    from concourse.bass_utils import run_bass_kernel_spmd

    x, norm_in_w, w_in, sinks_a, q_a_norm_w, w_q_b, kv_a_norm_w, w_kv_b, w_out, final_norm_w = (
        np.asarray(a) for a in (x, norm_in_w, w_in, sinks_a, q_a_norm_w, w_q_b, kv_a_norm_w, w_kv_b, w_out, final_norm_w))
    arrays = {
        "w_stream": laid_out_weights(w_in, w_q_b, w_kv_b, w_out),
        "x_t": np.ascontiguousarray(x[0].T.reshape(8, 2, P, SEQ).transpose(0, 2, 1, 3).reshape(8, P, CE)),
        "x_nat": np.ascontiguousarray(x),
        "gains": np.ascontiguousarray(np.concatenate(
            [norm_in_w.reshape(K_IN, P).T, q_a_norm_w.reshape(CQ_T, P).T, kv_a_norm_w.reshape(CKV_T, P).T,
             np.broadcast_to(sinks_a[None, :], (P, A_HEADS))], axis=1)),
        "final_w": np.ascontiguousarray(np.broadcast_to(final_norm_w[None, :], (P, D_MODEL))),
        "tables": rotary_tables(),
    }
    nc = bacc.Bacc("TRN2", target_bir_lowering=False, num_devices=1)
    args = [nc.dram_tensor(name, a.shape, mybir.dt.from_np(a.dtype), kind="ExternalInput").ap() for name, a in arrays.items()]
    args.append(nc.dram_tensor("out", (1, SEQ, D_MODEL), F32, kind="ExternalOutput").ap())
    build(nc, *args)
    r = run_bass_kernel_spmd(nc, [arrays], core_ids=[0])
    return r.results[0]["out"]
```
